# Optimizing a Trainium2 kernel written in Bass

```python
import math
import jax, jax.numpy as jnp
from jax import lax
import numpy as np

D_MODEL = 1024
BATCH = 1
SEQ = 1024
DEPTH = 1
DEC_BATCH = 8
DEC_SEQ = 1
PAST_LEN = 2048
PAGE_SIZE = 128

HEADS_A = 16
KV_HEADS_A = 4
GROUP_A = HEADS_A // KV_HEADS_A
HEAD_DIM_A = D_MODEL // HEADS_A
WINDOW = 128
HEADS_B = 4
DK_B = D_MODEL // 2 // HEADS_B
DV_B = D_MODEL // HEADS_B
GATE_RANK = 16
GATE_TEMP = 16.0
GLA_CHUNK = 64
PEER_HEADS = 8
N_KEYS = 128
N_EXPERTS = N_KEYS * N_KEYS
PEER_TOPK = 16
PEER_DKEY = 256
PEER_DHALF = PEER_DKEY // 2
PEER_BLOCK = 256
EPS = 1e-6
COLS = (HEADS_A * HEAD_DIM_A, KV_HEADS_A * HEAD_DIM_A, KV_HEADS_A * HEAD_DIM_A,
        HEADS_B * DK_B, HEADS_B * DK_B, HEADS_B * DV_B, HEADS_B * DV_B,
        GATE_RANK, D_MODEL, D_MODEL)
IN_COLS = sum(COLS)

kernel_name = "hybrid_swa_gla_peer_step"

def rmsnorm(x, g):
    xf = x.astype(jnp.float32)
    y = xf * lax.rsqrt(jnp.mean(xf * xf, axis=-1, keepdims=True) + EPS) * g.astype(jnp.float32)
    return y.astype(x.dtype)

def alibi_slopes():
    return 2.0 ** (-8.0 * jnp.arange(1, HEADS_A + 1, dtype=jnp.float32) / HEADS_A)

def swa_sink_attend(q, k, v, q_pos, k_pos, sinks):
    f32 = jnp.float32
    s = jnp.einsum('btkgd,bskd->bkgts', q.astype(f32), k.astype(f32)) * (HEAD_DIM_A ** -0.5)
    dist = q_pos[:, None] - k_pos[None, :]
    valid = (dist >= 0) & (dist < WINDOW) & (k_pos[None, :] >= 0)
    slopes = alibi_slopes().reshape(KV_HEADS_A, GROUP_A)
    s = s - slopes[None, :, :, None, None] * dist.astype(f32)
    s = jnp.where(valid, s, -jnp.inf)
    sink = sinks.astype(f32).reshape(KV_HEADS_A, GROUP_A)[None, :, :, None, None]
    m = jnp.maximum(jnp.max(s, axis=-1, keepdims=True), sink)
    p = jnp.exp(s - m)
    denom = jnp.sum(p, axis=-1, keepdims=True) + jnp.exp(sink - m)
    o = jnp.einsum('bkgts,bskd->btkgd', p / denom, v.astype(f32))
    return o.astype(v.dtype)

def banded_swa(q, k, v, sinks):
    B, L = q.shape[:2]
    nb = L // WINDOW
    qb = q.reshape(B, nb, WINDOW, KV_HEADS_A, GROUP_A, HEAD_DIM_A).swapaxes(0, 1)

    def band(t):
        tp = jnp.pad(t, ((0, 0), (WINDOW, 0), (0, 0), (0, 0))).reshape(B, nb + 1, WINDOW, KV_HEADS_A, HEAD_DIM_A)
        return jnp.concatenate([tp[:, :-1], tp[:, 1:]], axis=2).swapaxes(0, 1)

    kb, vb = band(k), band(v)

    def one_block(args):
        j, qj, kj, vj = args
        q_pos = j * WINDOW + jnp.arange(WINDOW, dtype=jnp.int32)
        k_pos = (j - 1) * WINDOW + jnp.arange(2 * WINDOW, dtype=jnp.int32)
        return swa_sink_attend(qj, kj, vj, q_pos, k_pos, sinks)

    o = lax.map(one_block, (jnp.arange(nb, dtype=jnp.int32), qb, kb, vb))
    return o.swapaxes(0, 1).reshape(B, L, KV_HEADS_A, GROUP_A, HEAD_DIM_A)

def gla_recurrent(q, k, v, log_a, S0, chunk):
    f32 = jnp.float32
    B, L, H, DK = q.shape
    DV = v.shape[-1]
    n = L // chunk

    def to_chunks(t):
        return t.astype(f32).reshape(B, n, chunk, H, t.shape[-1]).transpose(1, 0, 3, 2, 4)

    causal = jnp.tril(jnp.ones((chunk, chunk), dtype=bool))

    def step(S, inp):
        qc, kc, vc, ac = inp
        b = jnp.cumsum(ac, axis=2)
        diff = b[:, :, :, None, :] - b[:, :, None, :, :]
        decay = jnp.exp(jnp.where(causal[:, :, None], diff, -jnp.inf))
        scores = jnp.einsum('bhtd,bhsd,bhtsd->bhts', qc, kc, decay)
        o = jnp.einsum('bhts,bhsv->bhtv', scores, vc) + jnp.einsum('bhtd,bhdv->bhtv', qc * jnp.exp(b), S)
        b_last = b[:, :, -1:, :]
        S = jnp.exp(b_last[:, :, 0, :])[..., None] * S + jnp.einsum('bhsd,bhsv->bhdv', kc * jnp.exp(b_last - b), vc)
        return S, o

    S, o = lax.scan(step, S0.astype(f32), (to_chunks(q), to_chunks(k), to_chunks(v), to_chunks(log_a)))
    o = o.transpose(1, 0, 3, 2, 4).reshape(B, L, H, DV)
    return o, S

def peer(h, peer_wq, peer_subkeys, peer_u, peer_v):
    f32 = jnp.float32
    D = h.shape[-1]
    xt = h.reshape(-1, D)
    T = xt.shape[0]
    blk = math.gcd(T, PEER_BLOCK)
    xb = xt.reshape(T // blk, blk, D)

    def one_block(xk):
        q = (xk @ peer_wq).astype(f32).reshape(blk, PEER_HEADS, 2, PEER_DHALF)
        s = jnp.einsum('thcd,hcnd->thcn', q, peer_subkeys.astype(f32))
        val, idx = lax.top_k(s, PEER_TOPK)
        cand = (val[:, :, 0, :, None] + val[:, :, 1, None, :]).reshape(blk, PEER_HEADS, PEER_TOPK * PEER_TOPK)
        cidx = (idx[:, :, 0, :, None] * N_KEYS + idx[:, :, 1, None, :]).reshape(blk, PEER_HEADS, PEER_TOPK * PEER_TOPK)
        sv, si = lax.top_k(cand, PEER_TOPK)
        eidx = jnp.take_along_axis(cidx, si, axis=-1)
        g = jax.nn.softmax(sv, axis=-1)
        ue = jnp.take(peer_u, eidx, axis=0)
        act = jax.nn.gelu(jnp.einsum('thkd,td->thk', ue.astype(f32), xk.astype(f32)), approximate=False)
        ve = jnp.take(peer_v, eidx, axis=0)
        return jnp.einsum('thk,thkd->td', g * act, ve.astype(f32)).astype(h.dtype)

    return lax.map(one_block, xb).reshape(h.shape)

def layer(x, prompt_mode, k_prev, v_prev, S0, norm1_g, w_in, w_gla_gate, b_gla_gate, attn_sinks,
          gla_norm_g, w_out, norm2_g, peer_wq, peer_subkeys, peer_u, peer_v):
    f32 = jnp.float32
    B, L, D = x.shape
    n1 = rmsnorm(x, norm1_g)
    proj = n1 @ w_in
    split_idx = np.cumsum(COLS)[:-1].tolist()
    qa, ka, va, qb, kb, vb, rb, zb, ga, gb = jnp.split(proj, split_idx, axis=-1)
    qa = qa.reshape(B, L, KV_HEADS_A, GROUP_A, HEAD_DIM_A)
    ka = ka.reshape(B, L, KV_HEADS_A, HEAD_DIM_A)
    va = va.reshape(B, L, KV_HEADS_A, HEAD_DIM_A)
    if prompt_mode:
        oa = banded_swa(qa, ka, va, attn_sinks)
        k_all, v_all = ka, va
    else:
        k_all = jnp.concatenate([k_prev.astype(ka.dtype), ka], axis=1)
        v_all = jnp.concatenate([v_prev.astype(va.dtype), va], axis=1)
        q_pos = PAST_LEN + jnp.arange(L, dtype=jnp.int32)
        k_pos = PAST_LEN - WINDOW + jnp.arange(WINDOW + L, dtype=jnp.int32)
        oa = swa_sink_attend(qa, k_all, v_all, q_pos, k_pos, attn_sinks)
    new_k = k_all[:, -WINDOW:]
    new_v = v_all[:, -WINDOW:]
    oa = oa.reshape(B, L, D)
    log_a = jax.nn.log_sigmoid((zb @ w_gla_gate + b_gla_gate).astype(f32)) / GATE_TEMP
    log_a = log_a.reshape(B, L, HEADS_B, DK_B)
    qg = qb.reshape(B, L, HEADS_B, DK_B).astype(f32) * (DK_B ** -0.5)
    kg = kb.reshape(B, L, HEADS_B, DK_B)
    vg = vb.reshape(B, L, HEADS_B, DV_B)
    og, S_new = gla_recurrent(qg, kg, vg, log_a, S0, math.gcd(L, GLA_CHUNK))
    og = rmsnorm(og, gla_norm_g) * jax.nn.silu(rb.reshape(B, L, HEADS_B, DV_B).astype(f32))
    og = og.reshape(B, L, D).astype(x.dtype)
    u = jax.nn.sigmoid(ga) * oa + jax.nn.sigmoid(gb) * og
    x = x + u @ w_out
    x = x + peer(rmsnorm(x, norm2_g), peer_wq, peer_subkeys, peer_u, peer_v)
    return x, new_k, new_v, S_new

def setup_inputs(seed: int = 0) -> dict:
    key = jax.random.key(seed)
    ks = jax.random.split(key, 20)
    f32 = jnp.float32
    nrm = lambda k, shape, scale: jax.random.normal(k, shape, f32) * scale
    return {
        "x_prompt": nrm(ks[0], (BATCH, SEQ, D_MODEL), 1.0),
        "x_sample": nrm(ks[1], (DEC_BATCH, DEC_SEQ, D_MODEL), 1.0),
        "cache_k_win": nrm(ks[2], (DEPTH, DEC_BATCH, WINDOW, KV_HEADS_A, HEAD_DIM_A), 1.0),
        "cache_v_win": nrm(ks[3], (DEPTH, DEC_BATCH, WINDOW, KV_HEADS_A, HEAD_DIM_A), 1.0),
        "state_gla": nrm(ks[4], (DEPTH, DEC_BATCH, HEADS_B, DK_B, DV_B), 1.0),
        "norm1_g": 1.0 + nrm(ks[5], (DEPTH, D_MODEL), 0.05),
        "w_in": nrm(ks[6], (DEPTH, D_MODEL, IN_COLS), D_MODEL ** -0.5),
        "w_gla_gate": nrm(ks[7], (DEPTH, GATE_RANK, HEADS_B * DK_B), GATE_RANK ** -0.5),
        "b_gla_gate": nrm(ks[8], (DEPTH, HEADS_B * DK_B), 0.1),
        "attn_sinks": nrm(ks[9], (DEPTH, HEADS_A), 0.5),
        "gla_norm_g": 1.0 + nrm(ks[10], (DEPTH, DV_B), 0.05),
        "w_out": nrm(ks[11], (DEPTH, D_MODEL, D_MODEL), D_MODEL ** -0.5),
        "norm2_g": 1.0 + nrm(ks[12], (DEPTH, D_MODEL), 0.05),
        "peer_wq": nrm(ks[13], (DEPTH, D_MODEL, PEER_HEADS * PEER_DKEY), D_MODEL ** -0.5),
        "peer_subkeys": nrm(ks[14], (DEPTH, PEER_HEADS, 2, N_KEYS, PEER_DHALF), PEER_DHALF ** -0.5),
        "peer_u": nrm(ks[15], (DEPTH, N_EXPERTS, D_MODEL), D_MODEL ** -0.5),
        "peer_v": nrm(ks[16], (DEPTH, N_EXPERTS, D_MODEL), 0.5),
        "final_norm_g": 1.0 + nrm(ks[17], (D_MODEL,), 0.05),
    }

def reference(x_prompt, x_sample, cache_k_win, cache_v_win, state_gla, norm1_g, w_in, w_gla_gate,
              b_gla_gate, attn_sinks, gla_norm_g, w_out, norm2_g, peer_wq, peer_subkeys, peer_u, peer_v,
              final_norm_g):
    y_p, y_s = x_prompt, x_sample
    kp_l, vp_l, sp_l, ks_l, vs_l, ss_l = [], [], [], [], [], []
    for l in range(DEPTH):
        w = (norm1_g[l], w_in[l], w_gla_gate[l], b_gla_gate[l], attn_sinks[l], gla_norm_g[l],
             w_out[l], norm2_g[l], peer_wq[l], peer_subkeys[l], peer_u[l], peer_v[l])
        S0_p = jnp.zeros((x_prompt.shape[0], HEADS_B, DK_B, DV_B), jnp.float32)
        y_p, kp, vp, sp = layer(y_p, True, None, None, S0_p, *w)
        y_s, k_s, v_s, s_s = layer(y_s, False, cache_k_win[l], cache_v_win[l], state_gla[l], *w)
        kp_l.append(kp.astype(cache_k_win.dtype)); vp_l.append(vp.astype(cache_v_win.dtype))
        sp_l.append(sp.astype(state_gla.dtype))
        ks_l.append(k_s.astype(cache_k_win.dtype)); vs_l.append(v_s.astype(cache_v_win.dtype))
        ss_l.append(s_s.astype(state_gla.dtype))
    y_prompt = rmsnorm(y_p, final_norm_g)
    y_sample = rmsnorm(y_s, final_norm_g)
    return (y_prompt, y_sample, jnp.stack(kp_l), jnp.stack(vp_l), jnp.stack(sp_l),
            jnp.stack(ks_l), jnp.stack(vs_l), jnp.stack(ss_l))


_drawn_inputs = setup_inputs


def setup_inputs(seed=0):
    import zlib

    import numpy as np

    out = dict(_drawn_inputs(seed))
    spreads = {}
    factors = {}
    for name, (base, spread) in spreads.items():
        noise = np.random.default_rng([zlib.crc32(name.encode()), seed]).standard_normal(out[name].shape)
        drawn = base * np.exp(spread * noise) if base else spread * noise
        out[name] = __import__('jax').numpy.asarray(drawn.astype(out[name].dtype))
    for name, factor in factors.items():
        out[name] = (out[name] * factor).astype(out[name].dtype)
    return out
```

```python
import numpy as np
import concourse.bass as bass
from concourse import mybir
from contextlib import ExitStack

P = 128
D = 1024
KC = D // P
SEQ = 1024
NS = 8
TILES = SEQ // P
CHUNKS = 2
TC = TILES // CHUNKS
CT = TC * P
ST = TC
HA, KVH, HD, W = 16, 4, 64, 128
HB, DK, DV = 4, 128, 256
RANK = 16
GATE_TEMP = 16.0
EPS = 1e-6
PH, NK, TOPK = 8, 128, 16
NE = NK * NK
PAIRS = PH * TOPK
HC = 2 * PH
UC = 256
LV = 7
NEG = -1.0e30

UNITS = ([("fm", i) for i in range(9)] + [("va", 0)] + [("vb", i) for i in range(4)]
         + [("ga", i) for i in range(4)] + [("rb", i) for i in range(4)] + [("gb", i) for i in range(4)]
         + [("wo", i) for i in range(4)] + [("wq", i) for i in range(8)])
NU = len(UNITS)
WR = 2
FMB = 19
SLOTS = 16
GROUPS = PAIRS // SLOTS
N_OUT = 3 + 1 + 2 + 1

C_ID, C_DIST, C_RESET, C_MASK = 0, 128, 384, 512
C_IOTA = C_MASK + 8 * 128
C_DIST_S = C_IOTA + 16
C_SLOPE_S = C_DIST_S + 128
C_END = C_SLOPE_S + 1


def slopes():
    return [2.0 ** (-8.0 * (h + 1) / HA) for h in range(HA)]


def constants():
    c = np.zeros((P, C_END), np.float32)
    i = np.arange(P)
    c[:, C_ID:C_ID + P] = np.eye(P)
    dist = i[:, None] + P - np.arange(2 * P)[None, :]
    c[:, C_DIST:C_DIST + 2 * P] = np.where((dist >= 0) & (dist < W), -dist, NEG)
    c[:, C_RESET:C_RESET + P] = 1.0
    for l in range(LV):
        m = (P // 2) >> l
        s, t = i[:, None], i[None, :]
        c[:, C_MASK + l * P:C_MASK + (l + 1) * P] = (t // (2 * m) == s // (2 * m)) & (t % (2 * m) >= m) & (s % (2 * m) < m)
    c[:, C_MASK + LV * P:C_MASK + (LV + 1) * P] = np.eye(P)
    c[:, C_IOTA:C_IOTA + 16] = np.arange(16)
    c[:, C_DIST_S:C_DIST_S + P] = -(P - 1 - i)[None, :]
    c[:, C_SLOPE_S] = np.array(slopes())[i % HA]
    return c


class Signal:

    def __init__(self, sem, keys):
        self.sem, self.keys, self.n = sem, {k: i + 1 for i, k in enumerate(keys)}, 0

    def at(self, key):
        return self.keys[key]

    def did(self, key):
        self.n += 1
        assert self.keys[key] == self.n, (key, self.keys[key], self.n)
        return 1


def tiles_of(c):
    return [(t, P) for t in range(TC)] + ([(ST, NS)] if c == 0 else [])


def pair_jobs(c):
    return [(0, 2, P), (2, 2, P)] + ([(ST, 1, NS)] if c == 0 else [])


def psum_jobs():
    jobs = []
    for c in range(CHUNKS):
        for t, _ in tiles_of(c):
            jobs += [(("nT", c, t, g), "dve") for g in range(2)]
        for b in range(FMB):
            jobs.append((("fm", c, b), "act"))
        tm = lambda kind, u, eng: [((kind, c, u, p[0]), eng) for p in pair_jobs(c)]
        jobs += tm("va", 0, "act")
        for n in range(HA // 4 * TC + 2):
            if n < 4 * TC:
                if n % 4 == 0:
                    jobs += tm("vb", n // 4, "act")
                jobs += [(("S", c, n, g), "dve") for g in range(2)]
            if 1 <= n <= 4 * TC:
                jobs += [(("PT", c, n - 1, g), "act") for g in range(2)]
            if n >= 2:
                jobs.append((("O", c, n - 2), "dve"))
        if c == 0:
            jobs += [(("sS",), "dve"), (("sST",), "dve"), (("sPT",), "dve"), (("sO",), "dve"),
                     (("sOt", 0), "dve"), (("sOt", 1), "dve")]
        if c == CHUNKS - 1:
            jobs.append((("kwin",), "dve"))
        jobs += [(("gate", c, h), "dve") for h in range(HB)]
        if c == 0:
            jobs.append((("gateS",), "dve"))
        for n in range(2 * HB):
            for j in range(2):
                jobs += [(("L", c, n, j, g), "dve") for g in range(2)]
            jobs += [(("kdT", c, n), "act")]
            for p in pair_jobs(c):
                if (p[0] != 0) == n % 2:
                    jobs.append((("ga", c, n // 2, p[0]), "act"))
            for j in range(2):
                jobs += [(("og", c, n, j), "act"), (("st", c, n, j), "dve")]
        if c == 0:
            jobs.append((("kSt",), "dve"))
            for b in range(NS):
                jobs += [(("vB", b, g), "dve") for g in range(2)]
        for kind, eng in (("rb", "dve"), ("gb", "act")):
            for u in range(4):
                jobs += tm(kind, u, eng)
        for t, _ in tiles_of(c):
            jobs += [(("uT", c, t, g), "act") for g in range(2)]
        for u in range(4):
            jobs += tm("wo", u, "dve")
        for t, _ in tiles_of(c):
            jobs += [(("n2T", c, t, g), "act") for g in range(2)]
        for q in range(HC):
            jobs += [(("q", c, q), "act"), (("s", c, q), "dve")]
        if c == 0:
            jobs += [(("sR", g), "dve") for g in range(4)]
    return jobs


def sample_accumulations():
    return [("fmS",), ("ogS",), ("qS",)]


def build(nc, a, o):
    fp32, u32, bf16 = mybir.dt.float32, mybir.dt.uint32, mybir.dt.bfloat16
    ALU, ACT, AX = mybir.AluOpType, mybir.ActivationFunctionType, mybir.AxisListType
    SL = slopes()

    ctx = ExitStack()
    with ctx:
        def sb(name, shape, dt=fp32):
            return ctx.enter_context(nc.sbuf_tensor(name, shape, dt))

        def sem(name):
            return ctx.enter_context(nc.semaphore(name))

        cst = sb("cst", [P, C_END])
        big = sb("big", [P, SLOTS * D])
        nTb = sb("nTb", [P, KC * CT])
        arena = sb("arena", [P, 25 * 256])
        kaT = sb("kaT", [P, 2, P + CT])
        va = sb("va", [P, 1 + TC, KVH * HD])
        vaS = sb("vaS", [NS, KVH * HD])
        qbT = sb("qbT", [P, HB, CT])
        kbT = sb("kbT", [P, HB, CT])
        bTb = sb("bTb", [P, HB * CT])
        wring = sb("wring", [P, WR, KC, UC])
        Pbb = sb("Pbb", [P, 2 * 4 * 256])
        glag = sb("glag", [P, DV])
        state = sb("state", [P, HB, DV])
        scT = sb("scT", [P, 2, P])
        kdTok = sb("kdTok", [P, 2, P])
        val = sb("val", [P, 1 + TC, HC, TOPK])
        idx = sb("idx", [P, 1 + TC, HC, TOPK], u32)
        eidx = sb("eidx", [P, TILES, PAIRS], u32)
        gate = sb("gate", [P, TILES, PAIRS])
        gateS = sb("gateS", [NS, PAIRS])
        eidS = sb("eidS", [NS, PAIRS])
        g1c = sb("g1c", [P, KC])
        wz = sb("wz", [P, KC, RANK])
        zbT = sb("zbT", [RANK, CT])
        wg = sb("wg", [RANK, HB * DK])
        bg = sb("bg", [P, HB])
        nsink = sb("nsink", [P, HA])
        nsinkP = sb("nsinkP", [P, 1])
        nTs = sb("nTs", [P, KC, NS])
        fmS = sb("fmS", [P, FMB, NS])
        qz = sb("qz", [P, HB, NS, NS])
        st1 = sb("st1", [P, 1 + TC])
        rs1 = sb("rs1", [P, 1 + TC])
        stO = sb("stO", [P, 1 + TC, HB])
        rsO = sb("rsO", [P, 1 + TC, HB])
        mx = sb("mx", [P, 4, 4])
        nm = sb("nm", [P, 4, 4])
        sk = sb("sk", [P, 4, 4])
        rsum = sb("rsum", [P, 4, 4])
        esink = sb("esink", [P, 4, 4])
        rden = sb("rden", [P, 4, 4])
        smS = sb("smS", [P, 6])
        epst = sb("epst", [P, 1])
        yS = sb("yS", [P, HB, NS])
        tS = sb("tS", [P, HB, NS])
        aS = sb("aS", [P, HB, NS])
        zS = sb("zS", [P, NS])
        kSn = sb("kSn", [NS, KVH * HD])
        qSs = sb("qSs", [P, HC, NS])
        oS = sb("oS", [HD, P])
        gs = sb("gs", [P, PH])

        ident = cst[:, C_ID:C_ID + P]
        dist = cst[:, C_DIST:C_DIST + 2 * P]
        ones = cst[:, C_RESET:C_RESET + P]
        masks = cst[:, C_MASK:C_MASK + 8 * P].rearrange("p (l t) -> p l t", l=8)
        iota = cst[:, C_IOTA:C_IOTA + TOPK]
        distS = cst[:, C_DIST_S:C_DIST_S + P]
        slopeS = cst[:, C_SLOPE_S:C_SLOPE_S + 1]
        xh = big[:, 0:5 * D].rearrange("p (t d) -> p t d", t=5)
        oa = big[:, 5 * D:10 * D].rearrange("p (t d) -> p t d", t=5)
        vog = big[:, 10 * D:15 * D].rearrange("p (t d) -> p t d", t=5)
        s0 = [big[:, 15 * D:16 * D].rearrange("p (h d) -> p h d", h=HB),
              Pbb[:, 0:D].rearrange("p (h d) -> p h d", h=HB)]
        nT = nTb[:, :].rearrange("p (k t) -> p k t", k=KC)
        qaT = arena[:, 0:8 * CT].rearrange("p (b t) -> p b t", b=8)
        PT = arena[:, 4096:6144].rearrange("p (n g c) -> p n g c", n=2, g=2)
        Y = arena[:, 0:HB * CT].rearrange("p (h t) -> p h t", h=HB)
        Tt = arena[:, HB * CT:2 * HB * CT].rearrange("p (h t) -> p h t", h=HB)
        E = arena[:, 0:9 * 256].rearrange("p (l t) -> p l t", l=9)
        Qd = arena[:, 9 * 256:17 * 256].rearrange("p (l t) -> p l t", l=8)
        Kd = arena[:, 17 * 256:25 * 256].rearrange("p (l t) -> p l t", l=8)
        junkO = arena[:, 0:5 * D].rearrange("p (t h d) -> p t h d", t=5, h=HB)
        qh = arena[:, 5 * D:5 * D + 2 * CT].rearrange("p (n t) -> p n t", n=2)
        tmp = arena[:, 0:CT].rearrange("p (t n) -> p t n", t=TC)
        bT = bTb[:, :].rearrange("p (h t) -> p h t", h=HB)
        kTs = bTb[:, :].rearrange("p (q b s) -> p q b s", q=2, b=NS)
        keysT = bTb[:, :].rearrange("p (q n) -> p q n", q=HC)
        Pb = Pbb[:, :].rearrange("p (n i s) -> p n i s", n=2, i=4)
        vS = Pbb[:, :].rearrange("p (b c) -> p b c", b=NS)
        M1 = Pbb[:, 0:D].rearrange("p (l t) -> p l t", l=8)
        sig = Pbb[:, D:2 * D].rearrange("p (n i c) -> p n i c", n=2, i=2)
        cand = oa[:, 0:2, :].rearrange("p a d -> p (a d)").rearrange("p (h k) -> p h k", h=PH)
        cand2 = oa[:, 2:4, :].rearrange("p a d -> p (a d)").rearrange("p (h k) -> p h k", h=PH)
        onehot = Pbb[:, :].rearrange("p (h k j) -> p h k j", h=PH, k=TOPK)
        idxf = vog[:, 0, 0:HC * TOPK].rearrange("p (q k) -> p q k", q=HC)
        pairs = lambda lo: vog[:, 0, lo:lo + 2 * PAIRS].rearrange("p (a h k) -> p a h k", a=2, h=PH)
        posu = vog[:, 1, 0:PAIRS].bitcast(u32).rearrange("p (h k) -> p h k", h=PH)
        piu, pif, e01 = pairs(256).bitcast(u32), pairs(512), pairs(768)
        g2b = Pbb[:, D:2 * D]
        SsT, Ps, PsT = (arena[:, 4096 + i * P:4096 + (i + 1) * P] for i in range(3))

        bank = [ctx.enter_context(nc.psum_tensor(f"bank{i}", [P, 512], fp32)) for i in range(8)]
        RING = 6
        jobs = psum_jobs()
        full = Signal(sem("full"), [k for k, _ in jobs])
        evac = {e: Signal(sem(f"evac_{e}"), [k for k, who in jobs if who == e]) for e in ("act", "dve")}
        owner = dict(jobs)
        number = {k: i for i, (k, _) in enumerate(jobs)}
        acc_full = Signal(sem("acc_full"), [("fmS",), ("qS",)])
        acc_free = Signal(sem("acc_free"), sample_accumulations())

        def B(key):
            return bank[number[key] % RING]

        def room(pe, key):
            n = number[key] - RING
            if n >= 0:
                before = jobs[n][0]
                pe.wait_ge(evac[owner[before]].sem, evac[owner[before]].at(before))
            return B(key)

        def emptied(eng, key):
            eng.wait_ge(evac[owner[key]].sem, evac[owner[key]].at(key))

        def filled(eng, key):
            eng.wait_ge(full.sem, full.at(key))
            return B(key)

        CC = range(CHUNKS)
        both = [(c, t) for c in CC for t, _ in tiles_of(c)]
        NQ = 4 * TC
        d_cst, d_par = sem("d_cst"), sem("d_par")
        d_x = [sem(f"d_x{c}") for c in CC]
        d_w = [sem(f"d_w{i}") for i in range(WR)]
        d_kv = sem("d_kv")
        d_vS = sem("d_vS")
        d_s0 = [sem(f"d_s0{i}") for i in range(2)]
        d_keys = [sem(f"d_keys{c}") for c in CC]
        d_g2 = [sem(f"d_g2{c}") for c in CC]
        d_scr = [sem(f"d_scr{c}") for c in CC]
        d_out = sem("d_out")
        d_st = [sem(f"d_st{i}") for i in range(2)]
        init = sem("init")
        ss1 = Signal(sem("ss1"), [(c, i) for c in CC for i in range(2)])
        n_tok = Signal(sem("n_tok"), both)
        nm_ready = Signal(sem("nm_ready"), [(c, n) for c in CC for n in range(NQ)])
        p_ready = Signal(sem("p_ready"), [(c, n) for c in CC for n in range(NQ)])
        smx = Signal(sem("smx"), ["nm", "p"])
        smp = Signal(sem("smp"), ["p"])
        y_ready = Signal(sem("y_ready"), [*CC])
        t_ready = Signal(sem("t_ready"), [*CC])
        aS_in = sem("aS_in")
        aS_out = sem("aS_out")
        NG = 2 * HB
        gk = [(c, n) for c in CC for n in range(NG)]
        d_ready = Signal(sem("d_ready"), gk)
        e_ready = Signal(sem("e_ready"), gk)
        q_ready = Signal(sem("q_ready"), gk)
        k_ready = Signal(sem("k_ready"), gk)
        sc_ready = Signal(sem("sc_ready"), [(c, n, j) for c, n in gk for j in range(2)])
        s0a = Signal(sem("s0a"), range(NS))
        s0n = Signal(sem("s0n"), range(NS))
        ogb = Signal(sem("ogb"), range(NS))
        fmz = sem("fmz")
        knew = sem("knew")
        gates_k = [(k, c, u, p[0]) for c in CC for k in ("ga", "rb", "gb") for u in range(4) for p in pair_jobs(c)]
        sig_ready = Signal(sem("sig_ready"), gates_k)
        sig_used = Signal(sem("sig_used"), gates_k)
        rb_mul = Signal(sem("rb_mul"), [k for k in gates_k if k[0] == "rb"])
        ssO = Signal(sem("ssO"), [*CC])
        rstdO = Signal(sem("rstdO"), [*CC])
        h_ready = Signal(sem("h_ready"), [*CC])
        n2_ready = Signal(sem("n2_ready"), both)
        n2_all = Signal(sem("n2_all"), [*CC])
        qS_ready = sem("qS_ready")
        sv_ready = Signal(sem("sv_ready"), [*CC])
        ex_ready = Signal(sem("ex_ready"), [*CC])
        routed = Signal(sem("routed"), [*CC])
        outs = Signal(sem("outs"), ["kSn", "kwin", "state"])
        gate_used = {k: i for i, k in enumerate(gates_k)}

        def unit_end(c, i):
            kind, u = UNITS[i]
            if kind in ("fm", "wq"):
                return ("fm" if kind == "fm" else "q", c, 2 * u + 1)
            return (kind, c, u, pair_jobs(c)[-1][0])



        ring = [big[:, r * D:(r + 1) * D] for r in range(SLOTS)]
        n2t, ht = nTb[:, 0:D], nTb[:, D:2 * D]
        acc = [nTb[:, 2 * D:3 * D], nTb[:, 3 * D:4 * D]]
        diag = [arena[:, k * P:(k + 1) * P] for k in range(SLOTS // 2)]
        gfb = arena[:, D:2 * D]
        dots, act_g, wgt = (arena[:, 2 * D + i * P:2 * D + (i + 1) * P] for i in range(3))
        ysum = arena[:, 3 * D:4 * D]
        ysq = arena[:, 4 * D:5 * D]
        yout = arena[:, 5 * D:6 * D]
        ix = sb("ix", [P, 2, SLOTS], u32)
        dg = sb("dg", [P, SLOTS])
        zero = arena[:, 2 * D + 3 * P:2 * D + 5 * P].bitcast(bf16)
        ixS = sb("ixS", [P, NS], u32)
        gT = sb("gT", [P, NS])
        dS = sb("dS", [P, NS, 2])
        aT = sb("aT", [P, NS])
        wzS = sb("wzS", [P, NS, NS])
        fs = sb("fs", [P, 2])
        eidx_f = eidx[:, :, :].rearrange("p t k -> p (t k)")
        gate_f = gate[:, :, :].rearrange("p t k -> p (t k)")

        gathered = [sem(f"gathered{r}") for r in range(SLOTS)]
        slot_used = [sem(f"slot_used{r}") for r in range(SLOTS)]
        d_n2, d_h, d_gf, d_y = sem("d_n2"), sem("d_h"), sem("d_gf"), sem("d_y")
        n2_used, h_used = sem("n2_used"), sem("h_used")
        dots_ready, act_ready, wgt_ready = sem("dots_ready"), sem("act_ready"), sem("wgt_ready")
        diag_ready = sem("diag_ready")
        v_done, v_free = sem("v_done"), sem("v_free")
        y_sum, y_rms, y_out, y_free = sem("y_sum"), sem("y_rms"), sem("y_out"), sem("y_free")
        sx = {k: sem("sx_" + k) for k in ("T", "ix", "n2b", "dot", "gelu", "w", "v", "y", "rms", "out")}

        passed = {e: sem(f"passed_{e}") for e in ("pool", "act", "dve", "pe")}

        def hold(eng, name, s, value):
            eng.wait_ge(s, value)
            eng.sem_inc(passed[name], 1)

        def use(tile, phase, i, b):
            return tile * (2 * GROUPS) + (phase * GROUPS + b) + i * 2

        def experts_pool(pool):
            pool.wait_ge(routed.sem, routed.at(CHUNKS - 1))
            for c in CC:
                pool.wait_ge(d_scr[c], 64 if c == 0 else 32)
            for r in range(SLOTS):
                pool.sem_inc(slot_used[r], 1)
            with pool.Fori(0, TILES) as tile:
                for phase in range(2):
                    table = a["u"] if phase == 0 else a["v"]
                    with pool.Fori(0, GROUPS // 2) as i:
                        for b in range(2):
                            nc.gpsimd.tensor_copy(ix[:, b, :], eidx_f[:, bass.ds(tile * PAIRS + i * (2 * SLOTS) + b * SLOTS, SLOTS)])
                            pool.drain()
                            for r in range(SLOTS):
                                hold(pool, "pool", slot_used[r], use(tile, phase, i, b) + 1)
                                pool.indirect_dma_start(out=ring[r], out_offset=None, in_=table,
                                                        in_offset=bass.IndirectOffsetOnAxis(ap=ix[:, b, r:r + 1], axis=0))\
                                    .then_inc(gathered[r], 16)
            for r in range(SLOTS):
                pool.wait_ge(slot_used[r], TILES * 2 * GROUPS + 1)
            pool.wait_ge(sx["ix"], 1)
            for r in range(SLOTS):
                table = a["u"] if r < NS else a["v"]
                pool.indirect_dma_start(out=ring[r], out_offset=None, in_=table,
                                        in_offset=bass.IndirectOffsetOnAxis(ap=ixS[:, r % NS:r % NS + 1], axis=0))\
                    .then_inc(gathered[r], 16)
            pool.wait_ge(d_out, 16 * N_OUT)
            for i in range(2):
                pool.wait_ge(d_st[i], 16 * (NS // 2))

        def experts_sp(sp):
            sp.wait_ge(routed.sem, routed.at(CHUNKS - 1))
            for c in CC:
                sp.wait_ge(d_scr[c], 64 if c == 0 else 32)
            sp.dma_start(gfb, a["gf"].partition_broadcast(P)).then_inc(d_gf, 16)
            with sp.Fori(0, TILES) as tile:
                sp.wait_ge(n2_used, tile + 1)
                sp.dma_start(n2t, o["n2"][bass.ds(tile * P, P), :]).then_inc(d_n2, 16)
                sp.wait_ge(h_used, tile + 1)
                sp.dma_start(ht, o["h"][bass.ds(tile * P, P), :]).then_inc(d_h, 16)
                sp.wait_ge(y_out, tile + 1)
                sp.dma_start(o["yp"][bass.ds(tile * P, P), :], yout).then_inc(d_y, 16)
                sp.wait_ge(d_y, tile * 16 + 16)
                sp.sem_inc(y_free, 1)
            sp.wait_ge(n2_used, TILES + 1)
            sp.wait_ge(h_used, TILES + 1)
            sp.dma_start(n2t[0:NS, :], o["n2"][SEQ:SEQ + NS, :]).then_inc(d_n2, 16)
            sp.dma_start(ht[0:NS, :], o["h"][SEQ:SEQ + NS, :]).then_inc(d_h, 16)
            sp.wait_ge(sx["out"], 1)
            sp.dma_start(o["ys"], yout[0:NS, :]).then_inc(d_y, 16)
            sp.wait_ge(d_y, 16 * (TILES + 1))

        def experts_dve(dve):
            v = nc.vector
            TT, STT = v.tensor_tensor, v.scalar_tensor_tensor
            v.memset(zero[:, :], 0.0)
            v.memset(wzS[:, :, :], 0.0)
            dve.drain()
            dve.sem_inc(v_free, 1)
            dve.sem_inc(n2_used, 1)
            dve.sem_inc(h_used, 1)
            dve.wait_ge(d_gf, 16)
            with dve.Fori(0, TILES) as tile:
                hold(dve, "dve", d_n2, tile * 16 + 16)
                with dve.Fori(0, GROUPS // 2) as i:
                    for b in range(2):
                        for r in range(SLOTS):
                            dve.wait_ge(gathered[r], use(tile, 0, i, b) * 16 + 16)
                            v.tensor_tensor_reduce(out=ring[r], in0=ring[r], in1=n2t, scale=1.0, scalar=0.0, op0=ALU.mult, op1=ALU.add,
                                                   accum_out=dg[:, r:r + 1]).then_inc(slot_used[r], 1)
                        dve.drain()
                        v.tensor_copy(dots[:, bass.ds(i * (2 * SLOTS) + b * SLOTS, SLOTS)], dg[:, :])
                        dve.drain()
                dve.sem_inc(n2_used, 1)
                dve.sem_inc(dots_ready, 1)
                v.memset(acc[0], 0.0)
                v.memset(acc[1], 0.0)
                dve.drain()
                dve.wait_ge(act_ready, tile + 1)
                TT(wgt, act_g, gate_f[:, bass.ds(tile * PAIRS, PAIRS)], ALU.mult).then_inc(wgt_ready, 1)
                dve.drain()
                with dve.Fori(0, GROUPS // 2) as i:
                    for b in range(2):
                        for r in range(1, SLOTS, 2):
                            s = acc[(r // 2) % 2]
                            dve.wait_ge(slot_used[(r - 4) % SLOTS], use(tile, 1, i, b) + (2 if r >= 4 else 1))
                            dve.wait_ge(gathered[r], use(tile, 1, i, b) * 16 + 16)
                            STT(s, ring[r], wgt[:, bass.ds(i * (2 * SLOTS) + (b * SLOTS + r), 1)], s, ALU.mult, ALU.add)\
                                .then_inc(slot_used[r], 1)
                dve.drain()
                TT(ysum, acc[0], acc[1], ALU.add)
                dve.drain()
                dve.wait_ge(d_h, tile * 16 + 16)
                TT(ysum, ysum, ht, ALU.add)
                dve.drain()
                dve.sem_inc(h_used, 1)
                dve.wait_ge(v_done, tile + 1)
                for g in range(2):
                    TT(ysum[:, g * 512:(g + 1) * 512], bank[6 + g][:, :], ysum[:, g * 512:(g + 1) * 512], ALU.add)
                dve.drain()
                dve.sem_inc(v_free, 1)
                dve.sem_inc(y_sum, 1)
                dve.wait_ge(y_rms, tile + 1)
                v.reciprocal(fs[:, 1:2], fs[:, 1:2])
                dve.drain()
                dve.wait_ge(y_free, tile + 1)
                STT(yout, ysum, fs[:, 1:2], gfb, ALU.mult, ALU.mult).then_inc(y_out, 1)
                dve.drain()
            dve.wait_ge(sx["T"], 1)
            v.tensor_copy(ixS[:, :], bank[0][:, 0:NS])
            v.tensor_copy(gT[:, :], bank[0][:, NS:2 * NS])
            dve.drain()
            dve.sem_inc(sx["ix"], 1)
            for t in range(NS):
                dve.wait_ge(gathered[t], TILES * 2 * GROUPS * 16 + 16)
                for g in range(2):
                    n = 2 * t + g
                    dve.wait_ge(sx["n2b"], n + 1)
                    x = ring[t][:, g * 512:(g + 1) * 512]
                    v.tensor_tensor_reduce(out=x, in0=x, in1=bank[1 + n % 4][:, :], scale=1.0, scalar=0.0, op0=ALU.mult, op1=ALU.add,
                                           accum_out=dS[:, t, g:g + 1]).then_inc(sx["dot"], 1)
            dve.drain()
            TT(aT[:, :], dS[:, :, 0], dS[:, :, 1], ALU.add)
            dve.drain()
            dve.sem_inc(sx["dot"], 1)
            dve.wait_ge(sx["gelu"], 1)
            for t in range(NS):
                last = TT(wzS[:, t, t:t + 1], aT[:, t:t + 1], gT[:, t:t + 1], ALU.mult)
            dve.drain()
            dve.sem_inc(sx["w"], 1)
            dve.wait_ge(sx["v"], 1)
            dve.wait_ge(d_h, TILES * 16 + 16)
            for g in range(2):
                TT(ysum[0:NS, g * 512:(g + 1) * 512], bank[6 + g][0:NS, :], ht[0:NS, g * 512:(g + 1) * 512], ALU.add)
            dve.drain()
            dve.sem_inc(sx["y"], 1)
            dve.wait_ge(sx["rms"], 1)
            v.reciprocal(fs[0:NS, 1:2], fs[0:NS, 1:2])
            dve.wait_ge(y_free, TILES + 1)
            dve.drain()
            STT(yout[0:NS, :], ysum[0:NS, :], fs[0:NS, 1:2], gfb[0:NS, :], ALU.mult, ALU.mult).then_inc(sx["out"], 1)

        def experts_act(act):
            A = nc.scalar.activation
            act.sem_inc(y_free, 1)
            with act.Fori(0, TILES) as tile:
                act.wait_ge(dots_ready, tile + 1)
                A(act_g, dots, ACT.Gelu).then_inc(act_ready, 1)
                act.wait_ge(wgt_ready, tile + 1)
                with act.Fori(0, GROUPS // 2) as i:
                    for b in range(2):
                        for k in range(SLOTS // 2):
                            hold(act, "act", slot_used[2 * k], use(tile, 1, i, b) + 1)
                            A(diag[k], ident, ACT.Copy, scale=wgt[:, bass.ds(i * (2 * SLOTS) + (b * SLOTS + 2 * k), 1)])\
                                .then_inc(diag_ready, 1)
                act.wait_ge(y_sum, tile + 1)
                A(ysq, ysum, ACT.Square, accum_out=fs[:, 0:1])
                act.drain()
                A(fs[:, 1:2], fs[:, 0:1], ACT.Sqrt, scale=1.0 / D, bias=epst[:, 0:1]).then_inc(y_rms, 1)
                act.drain()
            act.wait_ge(sx["dot"], 2 * NS + 1)
            A(aT[:, :], aT[:, :], ACT.Gelu).then_inc(sx["gelu"], 1)
            act.wait_ge(sx["y"], 1)
            A(ysq[0:NS, :], ysum[0:NS, :], ACT.Square, accum_out=fs[0:NS, 0:1])
            act.drain()
            A(fs[0:NS, 1:2], fs[0:NS, 0:1], ACT.Sqrt, scale=1.0 / D, bias=epst[0:NS, 0:1]).then_inc(sx["rms"], 1)

        def experts_pe(pe):
            mm, tr = nc.tensor.matmul, nc.tensor.transpose
            with pe.Fori(0, TILES) as tile:
                pe.wait_ge(v_free, tile + 1)
                pe.wait_ge(wgt_ready, tile + 1)
                for g in range(2):
                    mm(bank[6 + g][:, :], zero[:, 0:P], zero[:, :], start=True, stop=False)
                with pe.Fori(0, GROUPS // 2) as i:
                    for b in range(2):
                        for k in range(SLOTS // 2):
                            r = 2 * k
                            pe.wait_ge(diag_ready, tile * (PAIRS // 2) + i * SLOTS + (b * (SLOTS // 2) + k + 1))
                            pe.wait_ge(gathered[r], use(tile, 1, i, b) * 16 + 16)
                            for g in range(2):
                                last = mm(bank[6 + g][:, :], diag[k], ring[r][:, g * 512:(g + 1) * 512], start=False, stop=False)
                            last.then_inc(slot_used[r], 1)
                for g in range(2):
                    last = mm(bank[6 + g][:, :], zero[:, 0:P], zero[:, :], start=False, stop=True)
                last.then_inc(v_done, 1)
            tr(bank[0][:, 0:NS], eidS[:, :], ident[0:NS, 0:NS])
            tr(bank[0][:, NS:2 * NS], gateS[:, :], ident[0:NS, 0:NS]).then_inc(sx["T"], 1)
            pe.wait_ge(d_n2, TILES * 16 + 16)
            for t in range(NS):
                for g in range(2):
                    n = 2 * t + g
                    if n >= 4:
                        pe.wait_ge(sx["dot"], n - 3)
                    mm(bank[1 + n % 4][:, :], ident[0:NS, t:t + 1].broadcast_to((NS, P)), n2t[0:NS, g * 512:(g + 1) * 512],
                       start=True, stop=True).then_inc(sx["n2b"], 1)
            pe.wait_ge(sx["w"], 1)
            pe.wait_ge(v_free, TILES + 1)
            for t in range(NS):
                pe.wait_ge(gathered[NS + t], TILES * 2 * GROUPS * 16 + 16)
                for g in range(2):
                    last = mm(bank[6 + g][0:NS, :], wzS[:, t, :], ring[NS + t][:, g * 512:(g + 1) * 512], start=(t == 0), stop=(t == NS - 1))
            last.then_inc(sx["v"], 1)

        def scTm(pe, c, n, j):
            pe.wait_ge(sc_ready.sem, sc_ready.at((c, n, j)))
            return scT[:, j, :]

        def sample_attention_pe(pe):
            mm, tr = nc.tensor.matmul, nc.tensor.transpose
            pe.wait_ge(knew, 1)
            ps = room(pe, ("sS",))
            for half in range(2):
                lo = half * 64
                for b in range(NS):
                    for Q in range(2):
                        q = 2 * Q + half
                        last = mm(ps[:, b * HA + q * 4:b * HA + q * 4 + 4], kTs[lo:lo + 64, Q, b, :], fmS[lo:lo + 64, 4 * Q:4 * Q + 4, b],
                                  start=True, stop=True)
                if half == 0:
                    pe.drain()
            last.then_inc(full.sem, full.did(("sS",)))
            emptied(pe, ("sS",))
            tr(room(pe, ("sST",))[:, 0:P], SsT, ident).then_inc(full.sem, full.did(("sST",)))
            pe.wait_ge(smx.sem, smx.at("p"))
            tr(room(pe, ("sPT",))[:, 0:P], Ps, ident).then_inc(full.sem, full.did(("sPT",)))
            emptied(pe, ("sPT",))
            pe.wait_ge(d_vS, 32)
            ps = room(pe, ("sO",))
            for b in range(NS):
                for q in range(KVH):
                    col = slice(b * HA + q * 4, b * HA + q * 4 + 4)
                    last = mm(ps[0:HD, col], vS[:, b, q * HD:(q + 1) * HD], PsT[:, col], start=True, stop=True)
            last.then_inc(full.sem, full.did(("sO",)))
            emptied(pe, ("sO",))
            for g in range(2):
                ps = room(pe, ("sOt", g))
                for i in range(8):
                    last = tr(ps[0:NS, i * HD:(i + 1) * HD], oS[:, 8 * g + i::HA], ident[0:HD, 0:HD])
                last.then_inc(full.sem, full.did(("sOt", g)))

        def sample_gla_pe(pe):
            mm, tr = nc.tensor.matmul, nc.tensor.transpose
            ps = room(pe, ("kSt",))
            for Q in range(2):
                last = tr(ps[0:NS, Q * P:(Q + 1) * P], fmS[:, 8 + Q, :], ident)
            last.then_inc(full.sem, full.did(("kSt",)))
            emptied(pe, ("vb", 0, 3, ST))
            pe.wait_ge(acc_free.sem, acc_free.at(("fmS",)))
            pe.wait_ge(fmz, 1)
            for g in range(2):
                mm(bank[6 + g][0:NS, :], zS[:, :], cst[:, 0:512], start=True, stop=False)
            for b in range(NS):
                for g in range(2):
                    ps = room(pe, ("vB", b, g))
                    mm(ps[:, :], ident[0:NS, b:b + 1].broadcast_to((NS, P)), vog[0:NS, ST, g * 512:(g + 1) * 512], start=True, stop=True)\
                        .then_inc(full.sem, full.did(("vB", b, g)))
                pe.wait_ge(s0n.sem, s0n.at(b))
                for h in range(HB):
                    last = mm(bank[6 + h // 2][0:NS, (h % 2) * DV:(h % 2 + 1) * DV], qz[:, h, b, :], s0[b % 2][:, h, :],
                              start=False, stop=False)
                if b == NS - 1:
                    for g in range(2):
                        last = mm(bank[6 + g][0:NS, :], zS[:, :], cst[:, 0:512], start=False, stop=True)
                last.then_inc(ogb.sem, ogb.did(b))

        def sample_attention_dve(dve):
            v = nc.vector
            TT, TS, STT = v.tensor_tensor, v.tensor_scalar, v.scalar_tensor_tensor
            done = lambda x, key: x.then_inc(evac["dve"].sem, evac["dve"].did(key))
            ps = filled(dve, ("sS",))
            done(TS(SsT, ps[:, 0:P], HD ** -0.5, None, ALU.mult), ("sS",))
            ps = filled(dve, ("sST",))
            done(STT(Ps, distS, slopeS, ps[:, 0:P], ALU.mult, ALU.add), ("sST",))
            dve.drain()
            v.tensor_reduce(smS[:, 0:1], Ps, axis=AX.X, op=ALU.max)
            dve.drain()
            STT(smS[:, 1:2], smS[:, 0:1], -1.0, nsinkP[:, :], ALU.mult, ALU.min)
            dve.drain()
            TT(smS[:, 2:3], smS[:, 1:2], nsinkP[:, :], ALU.subtract).then_inc(smx.sem, smx.did("nm"))
            dve.wait_ge(smp.sem, smp.at("p"))
            TT(smS[:, 5:6], smS[:, 3:4], smS[:, 4:5], ALU.add)
            dve.drain()
            v.reciprocal(smS[:, 5:6], smS[:, 5:6])
            dve.drain()
            TS(Ps, Ps, smS[:, 5:6], None, ALU.mult).then_inc(smx.sem, smx.did("p"))
            ps = filled(dve, ("sPT",))
            done(v.tensor_copy(PsT, ps[:, 0:P]), ("sPT",))
            ps = filled(dve, ("sO",))
            done(v.tensor_copy(oS[:, :], ps[0:HD, 0:P]), ("sO",))
            for g in range(2):
                ps = filled(dve, ("sOt", g))
                done(v.tensor_copy(oa[0:NS, ST, g * 512:(g + 1) * 512], ps[0:NS, :]), ("sOt", g))

        def sample_gla_dve(dve):
            v = nc.vector
            done = lambda x, key: x.then_inc(evac["dve"].sem, evac["dve"].did(key))
            ps = filled(dve, ("kSt",))
            done(v.tensor_copy(kSn[:, :], ps[0:NS, 0:KVH * HD]), ("kSt",))
            dve.drain()
            dve.sem_inc(outs.sem, outs.did("kSn"))
            for b in range(NS):
                dve.wait_ge(s0a.sem, s0a.at(b))
                for g in range(2):
                    key = ("vB", b, g)
                    ps = filled(dve, key)
                    for i in range(2):
                        h = 2 * g + i
                        s = s0[b % 2][:, h, :]
                        last = v.scalar_tensor_tensor(s, ps[:, i * DV:(i + 1) * DV], fmS[:, 14 + h, b:b + 1], s, ALU.mult, ALU.add)
                    done(last, key)
                dve.drain()
                dve.sem_inc(s0n.sem, s0n.did(b))
            dve.wait_ge(ogb.sem, ogb.at(NS - 1))
            for g in range(2):
                last = v.tensor_copy(vog[0:NS, ST, g * 512:(g + 1) * 512], bank[6 + g][0:NS, :])
            dve.drain()
            dve.sem_inc(acc_free.sem, acc_free.did(("ogS",)))

        def route(dve, c):
            v = nc.vector
            TT, TS = v.tensor_tensor, v.tensor_scalar
            for t, R in tiles_of(c):
                vv = val[0:R, t, :, :].rearrange("p (h c) k -> p h c k", c=2)
                sv = gateS[0:R, :] if R == NS else gate[:, c * TC + t, :]
                sv = sv.rearrange("p (h k) -> p h k", h=PH)
                cd, cd2, oh = cand[0:R], cand2[0:R], onehot[0:R]
                xf = idxf[0:R]
                v.tensor_copy(xf, idx[0:R, t, :, :])
                TT(cd.rearrange("p h (i j) -> p h i j", i=TOPK), vv[:, :, 0, :].rearrange("p h (k o) -> p h k o", o=1).broadcast_to((R, PH, TOPK, TOPK)),
                   vv[:, :, 1:2, :].broadcast_to((R, PH, TOPK, TOPK)), ALU.add)
                dve.drain()
                for h in range(PH):
                    v.max(sv[:, h, 0:8], cd[:, h, :])
                dve.drain()
                for h in range(PH):
                    v.max_index(posu[0:R, h, 0:8], sv[:, h, 0:8], cd[:, h, :])
                    v.match_replace(cd2[:, h, :], sv[:, h, 0:8], cd[:, h, :], -3.0e38)
                dve.drain()
                for h in range(PH):
                    v.max(sv[:, h, 8:16], cd2[:, h, :])
                dve.drain()
                for h in range(PH):
                    v.max_index(posu[0:R, h, 8:16], sv[:, h, 8:16], cd2[:, h, :])
                dve.drain()
                v.tensor_single_scalar(piu[0:R, 0], posu[0:R], 4, ALU.logical_shift_right)
                v.tensor_single_scalar(piu[0:R, 1], posu[0:R], TOPK - 1, ALU.bitwise_and)
                dve.drain()
                v.tensor_copy(pif[0:R], piu[0:R])
                x2 = xf.rearrange("p (h c) k -> p h c k", c=2)
                for half in range(2):
                    dve.drain()
                    TT(oh, iota[0:R, :].rearrange("p (a b k) -> p a b k", a=1, b=1).broadcast_to((R, PH, TOPK, TOPK)),
                       pif[0:R, half].rearrange("p h (k o) -> p h k o", o=1).broadcast_to((R, PH, TOPK, TOPK)), ALU.is_equal)
                    dve.drain()
                    TT(oh, oh, x2[:, :, half:half + 1, :].broadcast_to((R, PH, TOPK, TOPK)), ALU.mult)
                    dve.drain()
                    v.tensor_reduce(e01[0:R, half], oh, axis=AX.X, op=ALU.add)
                dve.drain()
                e = lambda i: e01[0:R, i].rearrange("p h k -> p (h k)")
                dst = eidS[0:R, :] if R == NS else eidx[:, c * TC + t, :]
                v.scalar_tensor_tensor(dst, e(0), float(NK), e(1), ALU.mult, ALU.add)
                TT(cd[:, :, 0:TOPK], sv, sv[:, :, 0:1].broadcast_to((R, PH, TOPK)), ALU.subtract)
                dve.drain()
                v.tensor_copy(sv, cd[:, :, 0:TOPK])
                dve.drain()
            dve.sem_inc(sv_ready.sem, sv_ready.did(c))
            dve.wait_ge(ex_ready.sem, ex_ready.at(c))
            for t, R in tiles_of(c):
                sv = gateS[0:R, :] if R == NS else gate[:, c * TC + t, :]
                sv = sv.rearrange("p (h k) -> p h k", h=PH)
                v.tensor_reduce(gs[0:R, :], sv, axis=AX.X, op=ALU.add)
                dve.drain()
                v.reciprocal(gs[0:R, :], gs[0:R, :])
                dve.drain()
                TT(sv, sv, gs[0:R, :].rearrange("p (h o) -> p h o", o=1).broadcast_to((R, PH, TOPK)), ALU.mult)
                dve.drain()
            dve.sem_inc(routed.sem, routed.did(c))

        block = ctx.enter_context(nc.Block())

        @block.sync
        def _(sp):
            sp.dma_start(xh[:, 0:TC, :], a["xp"][0:CT, :].rearrange("(t p) d -> p t d", p=P)).then_inc(d_x[0], 16)
            sp.dma_start(xh[0:NS, ST, :], a["xs"]).then_inc(d_x[0], 16)
            sp.dma_start(cst[:, :], a["cst"]).then_inc(d_cst, 16)
            sp.dma_start(g1c[:, :], a["g1c"]).then_inc(d_cst, 16)
            sp.dma_start(wz[:, :, :], a["wz"]).then_inc(d_cst, 16)
            for c in CC:
                for i, (kind, u) in enumerate(UNITS):
                    n = c * NU + i
                    if n >= WR:
                        last = unit_end(c, i - WR) if i >= WR else unit_end(c - 1, NU + i - WR)
                        sp.wait_ge(full.sem, full.at(last))
                    sp.dma_start(wring[:, n % WR, :, :].rearrange("p k c -> p (k c)"), a["w"][i]).then_inc(d_w[n % WR], 16)
                    if n == 0:
                        sp.dma_start(wg[:, :], a["wg"]).then_inc(d_par, 16)
                        sp.dma_start(bg[:, :], a["bg"]).then_inc(d_par, 16)
                        sp.dma_start(nsink[:, :], a["sinks"].partition_broadcast(P)).then_inc(d_par, 16)
                        sp.dma_start(nsinkP[:, :], a["sinksP"]).then_inc(d_par, 16)
                        sp.dma_start(glag[:, :], a["glag"].partition_broadcast(P)).then_inc(d_par, 16)
                        sp.dma_start(kTs[:, :, :, 0:W - 1], a["kTs"]).then_inc(d_kv, 16)
                if c + 1 < CHUNKS:
                    sp.wait_ge(d_scr[c], 64)
                    sp.dma_start(xh[:, 0:TC, :], a["xp"][(c + 1) * CT:(c + 2) * CT, :].rearrange("(t p) d -> p t d", p=P)).then_inc(d_x[c + 1], 16)
            experts_sp(sp)

        @block.gpsimd
        def _(pool):
            g = nc.gpsimd
            g.memset(st1[:, :], 1.0)
            g.memset(stO[:, :, :], 1.0)
            g.memset(kaT[:, :, 0:P], 0.0)
            g.memset(va[:, 0, :], 0.0)
            g.memset(state[:, :, :], 0.0)
            g.memset(qz[:, :, :, :], 0.0)
            g.memset(epst[:, :], EPS)
            g.memset(zS[:, :], 0.0)
            pool.drain()
            pool.sem_inc(init, 1)

            def ga_gate(c, u, p):
                p0, n, R = p
                key = ("ga", c, u, p0)
                pool.wait_ge(sig_ready.sem, sig_ready.at(key))
                x = oa[0:R, p0:p0 + n, u * UC:(u + 1) * UC]
                g.tensor_tensor(x, x, sig[0:R, gate_used[key] % 2, 0:n, :], ALU.mult).then_inc(sig_used.sem, sig_used.did(key))

            for c in CC:
                if c == 0:
                    pool.wait_ge(evac["act"].sem, evac["act"].at(("va", 0, 0, ST)))
                    pool.wait_ge(p_ready.sem, p_ready.at((0, NQ - 1)))
                    pool.wait_ge(full.sem, full.at(("PT", 0, NQ - 1, 1)))
                    pool.dma_start(vS[0:W - 1, :, :], a["vc"][:, 1:W, :].rearrange("b s c -> s b c")).then_inc(d_vS, 16)
                    pool.dma_start(vS[W - 1:W, :, :].rearrange("p b c -> p (b c)"), vaS[:, :]).then_inc(d_vS, 16)
                    pool.dma_start(o["ks"][:, 0:W - 1, :], a["kc"][:, 1:W, :]).then_inc(d_out, 16)
                    pool.dma_start(o["vs"][:, 0:W - 1, :], a["vc"][:, 1:W, :]).then_inc(d_out, 16)
                    pool.dma_start(o["vs"][:, W - 1, :], vaS[:, :]).then_inc(d_out, 16)
                for n in range(NG):
                    h, hf = n // 2, n % 2
                    pool.wait_ge(e_ready.sem, e_ready.at((c, n)))
                    if n >= 1:
                        pool.wait_ge(full.sem, full.at(("kdT", c, n - 1)))
                    kb = kbT[:, h:h + 1, hf * 256:(hf + 1) * 256].broadcast_to((P, 8, 256))
                    g.tensor_tensor(Kd, E[:, 1:9, :], kb, ALU.mult).then_inc(k_ready.sem, k_ready.did((c, n)))
                    for p in pair_jobs(c):
                        if (p[0] != 0) == n % 2:
                            ga_gate(c, n // 2, p)
                pool.dma_start(keysT, a["keysT"]).then_inc(d_keys[c], 16)
                if c == 0:
                    for b in range(NS):
                        if b == 0:
                            pool.wait_ge(sc_ready.sem, sc_ready.at((0, NG - 1, 1)))
                        if b >= 2:
                            pool.wait_ge(ogb.sem, ogb.at(b - 2))
                            pool.wait_ge(s0n.sem, s0n.at(b - 2))
                            pool.dma_start(o["ss"][b - 2].rearrange("h p d -> p h d"), s0[b % 2]).then_inc(d_st[b % 2], 16)
                            pool.wait_ge(d_st[b % 2], 16 * (b // 2))
                        pool.dma_start(s0[b % 2], a["s0"][b].rearrange("h p d -> p h d")).then_inc(d_s0[b % 2], 16)
                    for b in (NS - 2, NS - 1):
                        pool.wait_ge(s0n.sem, s0n.at(b))
                        pool.dma_start(o["ss"][b].rearrange("h p d -> p h d"), s0[b % 2]).then_inc(d_st[b % 2], 16)
                    pool.wait_ge(outs.sem, outs.at("kSn"))
                    pool.dma_start(o["ks"][:, W - 1, :], kSn[:, :]).then_inc(d_out, 16)
                else:
                    pool.wait_ge(outs.sem, outs.at("kwin"))
                    pool.dma_start(o["kp"], vog[:, 4, 0:KVH * HD]).then_inc(d_out, 16)
                    pool.dma_start(o["vp"], va[:, TC, :]).then_inc(d_out, 16)
                    pool.wait_ge(outs.sem, outs.at("state"))
                    pool.dma_start(o["sp"].rearrange("h p d -> p h d"), state[:, :, :]).then_inc(d_out, 16)
                for u in range(4):
                    for p0, n, R in pair_jobs(c):
                        key = ("rb", c, u, p0)
                        x = vog[0:R, p0:p0 + n, u * UC:(u + 1) * UC]
                        pool.wait_ge(rb_mul.sem, rb_mul.at(key))
                        g.tensor_tensor(x, x, sig[0:R, gate_used[key] % 2, 0:n, :], ALU.mult).then_inc(sig_used.sem, sig_used.did(key))
                        pool.drain()
                        gl = glag[0:R, :].rearrange("p (i d) -> p i d", i=1).broadcast_to((R, n, DV))
                        g.tensor_tensor(x, x, gl, ALU.mult)
                pool.drain()
                for u in range(4):
                    for p0, n, R in pair_jobs(c):
                        key = ("gb", c, u, p0)
                        x = vog[0:R, p0:p0 + n, u * UC:(u + 1) * UC]
                        y = oa[0:R, p0:p0 + n, u * UC:(u + 1) * UC]
                        pool.wait_ge(sig_ready.sem, sig_ready.at(key))
                        g.tensor_tensor(x, x, sig[0:R, gate_used[key] % 2, 0:n, :], ALU.mult)
                        pool.drain()
                        g.tensor_tensor(y, y, x, ALU.add).then_inc(sig_used.sem, sig_used.did(key))
                pool.drain()
                pool.dma_start(g2b, a["g2"].partition_broadcast(P)).then_inc(d_g2[c], 16)
                pool.wait_ge(h_ready.sem, h_ready.at(c))
                pool.dma_start(o["h"][c * CT:(c + 1) * CT, :].rearrange("(t p) d -> p t d", p=P), xh[:, 0:TC, :]).then_inc(d_scr[c], 16)
                pool.wait_ge(n2_all.sem, n2_all.at(c))
                pool.dma_start(o["n2"][c * CT:(c + 1) * CT, :].rearrange("(t p) d -> p t d", p=P), oa[:, 0:TC, :]).then_inc(d_scr[c], 16)
                if c == 0:
                    pool.dma_start(o["h"][SEQ:SEQ + NS, :], xh[0:NS, ST, :]).then_inc(d_scr[c], 16)
                    pool.dma_start(o["n2"][SEQ:SEQ + NS, :], oa[0:NS, ST, :]).then_inc(d_scr[c], 16)
            experts_pool(pool)

        @block.tensor
        def _(pe):
            mm, tr = nc.tensor.matmul, nc.tensor.transpose

            def weights(c, kind, u):
                n = c * NU + UNITS.index((kind, u))
                pe.wait_ge(d_w[n % WR], 16 * (n // WR + 1))
                return wring[:, n % WR, :, :]

            def token_major(c, kind, u, p, lhs, lhs_s):
                p0, n, R = p
                w = wring[:, (c * NU + UNITS.index((kind, u))) % WR, :, :]
                key = (kind, c, u, p0)
                ps = room(pe, key)
                for i in range(n):
                    for k in range(KC):
                        x = lhs_s[:, k, :] if R == NS else lhs[:, k, (p0 + i) * P:(p0 + i + 1) * P]
                        last = mm(ps[0:R, i * UC:(i + 1) * UC], x, w[:, k, :], start=(k == 0), stop=(k == KC - 1))
                last.then_inc(full.sem, full.did(key))
                return last

            def unit(c, kind, u):
                weights(c, kind, u)
                for p in pair_jobs(c):
                    token_major(c, kind, u, p, nT, nTs)

            def turn(key, src, t, R, g):
                ps = room(pe, key)
                for i in range(4):
                    k = 4 * g + i
                    last = tr(ps[:, i * R:(i + 1) * R], src[0:R, t, k * P:(k + 1) * P], ident[0:R, 0:R])
                last.then_inc(full.sem, full.did(key))

            pe.wait_ge(d_cst, 48)
            for c in CC:
                for t, R in tiles_of(c):
                    pe.wait_ge(n_tok.sem, n_tok.at((c, t)))
                    for g in range(2):
                        turn(("nT", c, t, g), oa, t, R, g)
                for t, R in tiles_of(c):
                    emptied(pe, ("nT", c, t, 1))
                for b in range(FMB):
                    if b < 18 and b % 2 == 0:
                        w = weights(c, "fm", b // 2)
                    ps = room(pe, ("fm", c, b))
                    M = P if b < 18 else RANK
                    lhs = [w[:, k, (b % 2) * P:(b % 2 + 1) * P] if b < 18 else wz[:, k, :] for k in range(KC)]
                    if c == 0:
                        for k in range(KC):
                            last = mm(bank[6][0:M, b * NS:(b + 1) * NS], lhs[k], nTs[:, k, :], start=(k == 0), stop=(k == KC - 1))
                        if b == FMB - 1:
                            last.then_inc(acc_full.sem, acc_full.did(("fmS",)))
                    for k in range(KC):
                        last = mm(ps[0:M, :], lhs[k], nT[:, k, :], start=(k == 0), stop=(k == KC - 1))
                    last.then_inc(full.sem, full.did(("fm", c, b)))
                unit(c, "va", 0)
                emptied(pe, ("fm", c, 9))
                for n in range(NQ + 2):
                    if n < NQ:
                        if n % 4 == 0:
                            unit(c, "vb", n // 4)
                        t, q = n // 4, n % 4
                        Q, half = q // 2, q % 2
                        lo = half * 64
                        for g in range(2):
                            ps = room(pe, ("S", c, n, g))
                            for i in range(2):
                                last = mm(ps[:, i * 256:(i + 1) * 256], qaT[lo:lo + 64, 4 * Q + 2 * g + i, t * P:(t + 1) * P],
                                          kaT[lo:lo + 64, Q, t * P:(t + 2) * P], start=True, stop=True)
                            last.then_inc(full.sem, full.did(("S", c, n, g)))
                    if 1 <= n <= NQ:
                        m = n - 1
                        pe.wait_ge(p_ready.sem, p_ready.at((c, m)))
                        for g in range(2):
                            ps = room(pe, ("PT", c, m, g))
                            for i in range(2):
                                for kb in range(2):
                                    j = 2 * i + kb
                                    last = tr(ps[:, j * P:(j + 1) * P], Pb[:, m % 2, 2 * g + i, kb * P:(kb + 1) * P], ident)
                            last.then_inc(full.sem, full.did(("PT", c, m, g)))
                    if n >= 2:
                        m = n - 2
                        t, q = m // 4, m % 4
                        if m == 0:
                            emptied(pe, ("va", c, 0, 2))
                        emptied(pe, ("PT", c, m, 1))
                        ps = room(pe, ("O", c, m))
                        for i in range(4):
                            for kb in range(2):
                                j = (2 * (i % 2) + kb) * P
                                last = mm(ps[:, i * HD:(i + 1) * HD], PT[:, m % 2, i // 2, j:j + P], va[:, t + kb, q * HD:(q + 1) * HD],
                                          start=(kb == 0), stop=(kb == 1))
                        last.then_inc(full.sem, full.did(("O", c, m)))
                if c == 0:
                    sample_attention_pe(pe)
                if c == CHUNKS - 1:
                    ps = room(pe, ("kwin",))
                    for Q in range(2):
                        last = tr(ps[:, Q * P:(Q + 1) * P], kaT[:, Q, CT:CT + P], ident)
                    last.then_inc(full.sem, full.did(("kwin",)))
                pe.wait_ge(d_par, 80)
                emptied(pe, ("fm", c, 18))
                for h in range(HB):
                    ps = room(pe, ("gate", c, h))
                    mm(ps[:, :], wg[:, h * DK:(h + 1) * DK], zbT[:, :], start=True, stop=True)\
                        .then_inc(full.sem, full.did(("gate", c, h)))
                if c == 0:
                    ps = room(pe, ("gateS",))
                    for h in range(HB):
                        last = mm(ps[:, h * NS:(h + 1) * NS], wg[:, h * DK:(h + 1) * DK], fmS[0:RANK, 18, :], start=True, stop=True)
                    last.then_inc(full.sem, full.did(("gateS",)))
                emptied(pe, ("vb", c, 3, 2))
                for n in range(NG):
                    h, hf = n // 2, n % 2
                    pe.wait_ge(q_ready.sem, q_ready.at((c, n)))
                    pe.wait_ge(k_ready.sem, k_ready.at((c, n)))
                    for j in range(2):
                        col = slice(j * P, (j + 1) * P)
                        tok = slice((2 * hf + j) * P, (2 * hf + j + 1) * P)
                        for g in range(2):
                            ps = room(pe, ("L", c, n, j, g))
                            for i in range(4):
                                l = 4 * g + i
                                kk, qq = (Kd[:, l, col], Qd[:, 1 + l, col]) if l < LV else (kbT[:, h, tok], qbT[:, h, tok])
                                last = mm(ps[:, i * P:(i + 1) * P], kk, qq, start=True, stop=True)
                            last.then_inc(full.sem, full.did(("L", c, n, j, g)))
                    ps = room(pe, ("kdT", c, n))
                    for j in range(2):
                        last = tr(ps[:, j * P:(j + 1) * P], Kd[:, 7, j * P:(j + 1) * P], ident)
                    last.then_inc(full.sem, full.did(("kdT", c, n)))
                    if n % 2 == 0:
                        weights(c, "ga", n // 2)
                    for p in pair_jobs(c):
                        if (p[0] != 0) == n % 2:
                            token_major(c, "ga", n // 2, p, nT, nTs)
                    emptied(pe, ("kdT", c, n))
                    for j in range(2):
                        t = 2 * hf + j
                        v = vog[:, t, h * DV:(h + 1) * DV]
                        ps = room(pe, ("og", c, n, j))
                        mm(ps[:, 0:DV], scTm(pe, c, n, j), v, start=True, stop=False)
                        if (n, j) != (0, 0):
                            before = (c, n, j - 1) if j else (c, n - 1, 1)
                            emptied(pe, ("st", *before))
                        mm(ps[:, 0:DV], Qd[:, 0, j * P:(j + 1) * P], state[:, h, :], start=False, stop=True)\
                            .then_inc(full.sem, full.did(("og", c, n, j)))
                        ps = room(pe, ("st", c, n, j))
                        mm(ps[:, 0:DV], kdTok[:, j, :], v, start=True, stop=True)\
                            .then_inc(full.sem, full.did(("st", c, n, j)))
                if c == 0:
                    sample_gla_pe(pe)
                for kind in ("rb", "gb"):
                    for u in range(4):
                        unit(c, kind, u)
                for i, (t, R) in enumerate(tiles_of(c)):
                    if i == 0:
                        pe.wait_ge(sig_used.sem, sig_used.at(("gb", c, 3, pair_jobs(c)[-1][0])))
                    for g in range(2):
                        turn(("uT", c, t, g), oa, t, R, g)
                for t, R in tiles_of(c):
                    emptied(pe, ("uT", c, t, 1))
                for u in range(4):
                    unit(c, "wo", u)
                for t, R in tiles_of(c):
                    pe.wait_ge(n2_ready.sem, n2_ready.at((c, t)))
                    for g in range(2):
                        turn(("n2T", c, t, g), oa, t, R, g)
                for t, R in tiles_of(c):
                    emptied(pe, ("n2T", c, t, 1))
                pe.wait_ge(d_keys[c], 16)
                for q in range(HC):
                    if q % 2 == 0:
                        w = weights(c, "wq", q // 2)
                    lhs = [w[:, k, (q % 2) * P:(q % 2 + 1) * P] for k in range(KC)]
                    ps = room(pe, ("q", c, q))
                    if c == 0:
                        if q == 0:
                            pe.wait_ge(acc_free.sem, acc_free.at(("ogS",)))
                        for k in range(KC):
                            last = mm(bank[6][:, q * NS:(q + 1) * NS], lhs[k], nTs[:, k, :], start=(k == 0), stop=(k == KC - 1))
                        if q == HC - 1:
                            last.then_inc(acc_full.sem, acc_full.did(("qS",)))
                    for k in range(KC):
                        last = mm(ps[:, :], lhs[k], nT[:, k, :], start=(k == 0), stop=(k == KC - 1))
                    last.then_inc(full.sem, full.did(("q", c, q)))
                    emptied(pe, ("q", c, q))
                    ps = room(pe, ("s", c, q))
                    for t in range(TC):
                        last = mm(ps[:, t * P:(t + 1) * P], qh[:, q % 2, t * P:(t + 1) * P], keysT[:, q, :], start=True, stop=True)
                    last.then_inc(full.sem, full.did(("s", c, q)))
                if c == 0:
                    pe.wait_ge(qS_ready, 1)
                    for g in range(4):
                        ps = room(pe, ("sR", g))
                        for i in range(4):
                            last = mm(ps[0:NS, i * P:(i + 1) * P], qSs[:, 4 * g + i, :], keysT[:, 4 * g + i, :], start=True, stop=True)
                        last.then_inc(full.sem, full.did(("sR", g)))
            experts_pe(pe)

        @block.scalar
        def _(act):
            A = nc.scalar.activation

            def copy(dst, key, src, scale=1.0):
                A(dst, src, ACT.Copy, scale=scale).then_inc(evac["act"].sem, evac["act"].did(key))

            def norm_stats(c, i, src, junk):
                for t, R in tiles_of(c):
                    A(junk[0:R, t, :], src[0:R, t, :], ACT.Square, accum_out=st1[0:R, t:t + 1])
                act.drain()
                A(rs1[:, :], st1[:, :], ACT.Sqrt, scale=1.0 / D, bias=epst[:, 0:1]).then_inc(ss1.sem, ss1.did((c, i)))

            def evac_turn(kind, c, g, t, R):
                key = (kind, c, t, g)
                ps = filled(act, key)
                dst = nT[:, 4 * g:4 * g + 4, t * P:(t + 1) * P] if R == P else nTs[:, 4 * g:4 * g + 4, :]
                copy(dst, key, ps[:, 0:4 * R].rearrange("p (k r) -> p k r", k=4))

            def sigmoid(kind, c, u, p):
                p0, n, R = p
                key = (kind, c, u, p0)
                ps = filled(act, key)
                s = gate_used[key]
                if s >= 2:
                    before = gates_k[s - 2]
                    act.wait_ge(sig_used.sem, sig_used.at(before))
                x = A(sig[0:R, s % 2, 0:n, :], ps[0:R, 0:n * UC].rearrange("p (i c) -> p i c", i=n), ACT.Sigmoid)
                x.then_inc(sig_ready.sem, sig_ready.did(key))
                if kind != "rb":
                    act.wait_ge(sig_ready.sem, sig_ready.at(key))
                    act.sem_inc(evac["act"].sem, evac["act"].did(key))

            def route_exp(c):
                act.wait_ge(sv_ready.sem, sv_ready.at(c))
                A(gate[:, c * TC:(c + 1) * TC, :], gate[:, c * TC:(c + 1) * TC, :], ACT.Exp)
                if c == 0:
                    A(gateS[:, :], gateS[:, :], ACT.Exp)
                act.drain()
                act.sem_inc(ex_ready.sem, ex_ready.did(c))

            act.wait_ge(init, 1)
            for c in CC:
                act.wait_ge(d_x[c], 32 if c == 0 else 16)
                if c:
                    act.wait_ge(d_scr[c - 1], 64)
                norm_stats(c, 0, xh, oa)
                for b in range(FMB):
                    ps = filled(act, ("fm", c, b))
                    if b < 8:
                        if b == 0 and c:
                            act.wait_ge(evac["dve"].sem, evac["dve"].at(("s", c - 1, HC - 1)))
                            if c == 1:
                                act.wait_ge(evac["dve"].sem, evac["dve"].at(("sR", 3)))
                        copy(qaT[:, b, :], ("fm", c, b), ps[:, :], HD ** -0.5)
                    elif b < 10:
                        if b == 8 and c:
                            A(kaT[:, :, 0:P], kaT[:, :, CT:CT + P], ACT.Copy)
                            act.drain()
                        copy(kaT[:, b - 8, P:P + CT], ("fm", c, b), ps[:, :])
                    elif b < 14:
                        copy(qbT[:, b - 10, :], ("fm", c, b), ps[:, :], DK ** -0.5)
                    elif b < 18:
                        copy(kbT[:, b - 14, :], ("fm", c, b), ps[:, :])
                    else:
                        copy(zbT[:, :], ("fm", c, b), ps[0:RANK, :])
                if c:
                    A(va[:, 0, :], va[:, TC, :], ACT.Copy)
                    act.drain()
                for p0, n, R in pair_jobs(c):
                    key = ("va", c, 0, p0)
                    ps = filled(act, key)
                    if R == P:
                        copy(va[:, 1 + p0:1 + p0 + n, :], key, ps[:, 0:n * UC].rearrange("p (i c) -> p i c", i=n))
                    else:
                        copy(vaS[:, :], key, ps[0:R, 0:UC])

                def vb(u):
                    for p0, n, R in pair_jobs(c):
                        key = ("vb", c, u, p0)
                        ps = filled(act, key)
                        copy(vog[0:R, p0:p0 + n, u * UC:(u + 1) * UC], key, ps[0:R, 0:n * UC].rearrange("p (i c) -> p i c", i=n))

                if c:
                    route_exp(c - 1)
                    act.wait_ge(routed.sem, routed.at(c - 1))
                for n in range(NQ + 1):
                    if n < NQ:
                        if n % 4 == 0:
                            vb(n // 4)
                    if n >= 1:
                        for g in range(2):
                            key = ("PT", c, n - 1, g)
                            if n >= 3:
                                act.wait_ge(full.sem, full.at(("O", c, n - 3)))
                            ps = filled(act, key)
                            copy(PT[:, (n - 1) % 2, g, :], key, ps[:, :])
                    if n < NQ:
                        act.wait_ge(nm_ready.sem, nm_ready.at((c, n)))
                        s = n % 4
                        for i in range(4):
                            A(Pb[:, n % 2, i, :], Pb[:, n % 2, i, :], ACT.Exp, bias=nm[:, s, i:i + 1], accum_out=rsum[:, s, i:i + 1])
                        A(esink[:, s, :], sk[:, s, :], ACT.Exp)
                        act.drain()
                        act.sem_inc(p_ready.sem, p_ready.did((c, n)))
                if c == 0:
                    act.wait_ge(smx.sem, smx.at("nm"))
                    A(Ps, Ps, ACT.Exp, bias=smS[:, 1:2], accum_out=smS[:, 3:4])
                    A(smS[:, 4:5], smS[:, 2:3], ACT.Exp)
                    act.drain()
                    act.sem_inc(smp.sem, smp.did("p"))
                act.wait_ge(y_ready.sem, y_ready.at(c))
                A(Tt, Y, ACT.Abs)
                if c == 0:
                    act.wait_ge(aS_in, 1)
                    A(tS[:, :, :], yS[:, :, :], ACT.Abs)
                act.drain()
                A(Tt, Tt, ACT.Exp, scale=-1.0)
                if c == 0:
                    A(tS[:, :, :], tS[:, :, :], ACT.Exp, scale=-1.0)
                act.drain()
                A(Tt, Tt, ACT.Ln, bias=1.0).then_inc(t_ready.sem, t_ready.did(c))
                if c == 0:
                    A(tS[:, :, :], tS[:, :, :], ACT.Ln, bias=1.0).then_inc(aS_out, 1)
                    act.wait_ge(aS_in, 2)
                    A(aS[:, :, :], yS[:, :, :], ACT.Exp, scale=1.0 / GATE_TEMP)
                for n in range(NG):
                    h, hf = n // 2, n % 2
                    act.wait_ge(d_ready.sem, d_ready.at((c, n)))
                    if n:
                        emptied(act, ("st", c, n - 1, 1))
                        act.wait_ge(q_ready.sem, q_ready.at((c, n - 1)))
                    A(E[:, 0, :], bT[:, h, hf * 256:(hf + 1) * 256], ACT.Exp, scale=1.0 / GATE_TEMP)
                    A(E[:, 1:9, :], E[:, 1:9, :], ACT.Exp, scale=1.0 / GATE_TEMP)
                    act.drain()
                    act.sem_inc(e_ready.sem, e_ready.did((c, n)))
                    key = ("kdT", c, n)
                    ps = filled(act, key)
                    if n:
                        act.wait_ge(full.sem, full.at(("st", c, n - 1, 1)))
                    copy(kdTok[:, :, :], key, ps[:, 0:2 * P].rearrange("p (j c) -> p j c", j=2))
                    for p in pair_jobs(c):
                        if (p[0] != 0) == n % 2:
                            sigmoid("ga", c, n // 2, p)
                    for j in range(2):
                        key = ("og", c, n, j)
                        ps = filled(act, key)
                        act.wait_ge(full.sem, full.at(("st", c, n, j)))
                        copy(vog[:, 2 * hf + j, h * DV:(h + 1) * DV], key, ps[:, 0:DV])
                if c == 0:
                    act.drain()
                    for b in range(NS):
                        act.wait_ge(d_s0[b % 2], 16 * (b // 2 + 1))
                        for h in range(HB):
                            last = A(s0[b % 2][:, h, :], s0[b % 2][:, h, :], ACT.Copy, scale=aS[:, h, b:b + 1])
                        act.drain()
                        act.sem_inc(s0a.sem, s0a.did(b))
                    act.wait_ge(acc_free.sem, acc_free.at(("ogS",)))
                emptied(act, ("st", c, NG - 1, 1))
                act.drain()
                for t, R in tiles_of(c):
                    for h in range(HB):
                        A(junkO[0:R, t, h, :], vog[0:R, t, h * DV:(h + 1) * DV], ACT.Square, accum_out=stO[0:R, t, h:h + 1])
                act.drain()
                A(rsO[:, :, :], stO[:, :, :], ACT.Sqrt, scale=1.0 / DV, bias=epst[:, 0:1]).then_inc(ssO.sem, ssO.did(c))
                for kind in ("rb", "gb"):
                    for u in range(4):
                        for p in pair_jobs(c):
                            sigmoid(kind, c, u, p)
                for t, R in tiles_of(c):
                    for g in range(2):
                        evac_turn("uT", c, g, t, R)
                act.wait_ge(h_ready.sem, h_ready.at(c))
                norm_stats(c, 1, xh, vog)
                for t, R in tiles_of(c):
                    for g in range(2):
                        evac_turn("n2T", c, g, t, R)
                for q in range(HC):
                    ps = filled(act, ("q", c, q))
                    if q >= 2:
                        act.wait_ge(full.sem, full.at(("s", c, q - 2)))
                    copy(qh[:, q % 2, :], ("q", c, q), ps[:, :])
            route_exp(CHUNKS - 1)
            experts_act(act)

        @block.vector
        def _(dve):
            v = nc.vector
            TT, TS, STT = v.tensor_tensor, v.tensor_scalar, v.scalar_tensor_tensor

            def done(x, key):
                return x.then_inc(evac["dve"].sem, evac["dve"].did(key))

            def rows(ap, R):
                return ap[0:R]

            dve.wait_ge(init, 1)
            dve.wait_ge(d_cst, 48)
            dve.wait_ge(d_par, 80)
            TS(nsink[:, :], nsink[:, :], -1.0, None, ALU.mult)
            TS(nsinkP[:, :], nsinkP[:, :], -1.0, None, ALU.mult)
            for c in CC:
                dve.wait_ge(ss1.sem, ss1.at((c, 0)))
                v.reciprocal(rs1[:, :], rs1[:, :])
                dve.drain()
                for t, R in tiles_of(c):
                    TS(oa[0:R, t, :], xh[0:R, t, :], rs1[0:R, t:t + 1], None, ALU.mult).then_inc(n_tok.sem, n_tok.did((c, t)))
                for t, R in tiles_of(c):
                    for g in range(2):
                        key = ("nT", c, t, g)
                        ps = filled(dve, key)
                        dst = nT[:, 4 * g:4 * g + 4, t * P:(t + 1) * P] if R == P else nTs[:, 4 * g:4 * g + 4, :]
                        gain = g1c[:, 4 * g:4 * g + 4].rearrange("p (k o) -> p k o", o=1).broadcast_to((P, 4, R))
                        if g == 0 and t == 0 and c:
                            pass
                        done(TT(dst, ps[:, 0:4 * R].rearrange("p (k r) -> p k r", k=4), gain, ALU.mult), key)
                if c:
                    route(dve, c - 1)
                if c == 0:
                    dve.wait_ge(acc_full.sem, acc_full.at(("fmS",)))
                    v.tensor_copy(fmS[:, 0:18, :], bank[6][:, 0:18 * NS].rearrange("p (b s) -> p b s", b=18))
                    v.tensor_copy(fmS[0:RANK, 18, :], bank[6][0:RANK, 18 * NS:19 * NS]).then_inc(acc_free.sem, acc_free.did(("fmS",)))
                    dve.drain()
                    dve.wait_ge(d_kv, 16)
                    for Q in range(2):
                        last = v.tensor_copy(kTs[:, Q, :, W - 1], fmS[:, 8 + Q, :])
                    last.then_inc(knew, 1)
                    for b in range(NS):
                        last = TS(qz[:, :, b, b], fmS[:, 10:14, b], DK ** -0.5, None, ALU.mult)
                    last.then_inc(fmz, 1)
                    dve.drain()
                for n in range(NQ + 2):
                    if n < NQ:
                        t, q, s = n // 4, n % 4, n % 4
                        for g in range(2):
                            key = ("S", c, n, g)
                            ps = filled(dve, key)
                            if g == 0 and n >= 2:
                                dve.wait_ge(full.sem, full.at(("PT", c, n - 2, 1)))
                            for i in range(2):
                                last = STT(Pb[:, n % 2, 2 * g + i, :], dist, SL[4 * q + 2 * g + i], ps[:, i * 256:(i + 1) * 256],
                                           ALU.mult, ALU.add)
                            done(last, key)
                        dve.drain()
                        if c == 0 and t == 0:
                            v.memset(Pb[:, n % 2, :, 0:P], NEG)
                            dve.drain()
                        v.tensor_reduce(mx[:, s, :], Pb[:, n % 2, :, :], axis=AX.X, op=ALU.max)
                        dve.drain()
                        STT(nm[:, s, :], mx[:, s, :], -1.0, nsink[:, 4 * q:4 * q + 4], ALU.mult, ALU.min)
                        dve.drain()
                        TT(sk[:, s, :], nm[:, s, :], nsink[:, 4 * q:4 * q + 4], ALU.subtract).then_inc(nm_ready.sem, nm_ready.did((c, n)))
                    if n >= 2:
                        m = n - 2
                        t, q, s = m // 4, m % 4, m % 4
                        key = ("O", c, m)
                        ps = filled(dve, key)
                        TT(rden[:, s, :], rsum[:, s, :], esink[:, s, :], ALU.add)
                        dve.drain()
                        v.reciprocal(rden[:, s, :], rden[:, s, :])
                        dve.drain()
                        done(TT(oa[:, t, q * 256:(q + 1) * 256].rearrange("p (i d) -> p i d", i=4),
                                ps[:, 0:256].rearrange("p (i d) -> p i d", i=4),
                                rden[:, s, :].rearrange("p (i o) -> p i o", o=1).broadcast_to((P, 4, HD)), ALU.mult), key)
                if c == 0:
                    sample_attention_dve(dve)
                if c == CHUNKS - 1:
                    ps = filled(dve, ("kwin",))
                    x = done(v.tensor_copy(vog[:, 4, 0:KVH * HD], ps[:, 0:KVH * HD]), ("kwin",))
                    dve.wait_ge(evac["dve"].sem, evac["dve"].at(("kwin",)))
                    dve.sem_inc(outs.sem, outs.did("kwin"))
                for h in range(HB):
                    ps = filled(dve, ("gate", c, h))
                    done(TS(Y[:, h, :], ps[:, :], bg[:, h:h + 1], None, ALU.add), ("gate", c, h))
                dve.drain()
                dve.sem_inc(y_ready.sem, y_ready.did(c))
                if c == 0:
                    ps = filled(dve, ("gateS",))
                    done(TT(yS[:, :, :], ps[:, 0:HB * NS].rearrange("p (h b) -> p h b", h=HB),
                            bg[:, :].rearrange("p (h o) -> p h o", o=1).broadcast_to((P, HB, NS)), ALU.add), ("gateS",))
                    dve.drain()
                    dve.sem_inc(aS_in, 1)
                dve.wait_ge(t_ready.sem, t_ready.at(c))
                STT(Y, Y, 0.0, Tt, ALU.min, ALU.subtract)
                if c == 0:
                    dve.wait_ge(aS_out, 1)
                    STT(yS[:, :, :], yS[:, :, :], 0.0, tS[:, :, :], ALU.min, ALU.subtract).then_inc(aS_in, 1)
                dve.drain()
                for h in range(HB):
                    for t in range(TC):
                        v.tensor_tensor_scan(bT[:, h, t * P:(t + 1) * P], ones, Y[:, h, t * P:(t + 1) * P], 0.0, ALU.mult, ALU.add)
                dve.drain()

                def differences(n):
                    h, hf = n // 2, n % 2
                    b = bT[:, h, hf * 256:(hf + 1) * 256]
                    for l in range(LV):
                        m = (P // 2) >> l
                        e = E[:, 1 + l, :].rearrange("p (n two m) -> p n two m", two=2, m=m)
                        bb = b.rearrange("p (n two m) -> p n two m", two=2, m=m)
                        edge = bb[:, :, 0, m - 1:m].broadcast_to((P, P // m, m))
                        TT(e[:, :, 1, :], bb[:, :, 1, :], edge, ALU.subtract)
                        TT(e[:, :, 0, :], edge, bb[:, :, 0, :], ALU.subtract)
                    b2 = b.rearrange("p (j t) -> p j t", j=2)
                    TT(E[:, 8, :].rearrange("p (j t) -> p j t", j=2), b2[:, :, P - 1:P].broadcast_to((P, 2, P)), b2, ALU.subtract)
                    dve.drain()
                    dve.sem_inc(d_ready.sem, d_ready.did((c, n)))

                for n in range(NG):
                    h, hf = n // 2, n % 2
                    if n == 0:
                        differences(0)
                    dve.wait_ge(e_ready.sem, e_ready.at((c, n)))
                    if n:
                        dve.wait_ge(full.sem, full.at(("og", c, n - 1, 1)))
                    qb = qbT[:, h:h + 1, hf * 256:(hf + 1) * 256].broadcast_to((P, 8, 256))
                    TT(Qd, E[:, 0:8, :], qb, ALU.mult).then_inc(q_ready.sem, q_ready.did((c, n)))
                    for j in range(2):
                        for g in range(2):
                            key = ("L", c, n, j, g)
                            ps = filled(dve, key)
                            done(TT(M1[:, 4 * g:4 * g + 4, :], ps[:, :].rearrange("p (l t) -> p l t", l=4), masks[:, 4 * g:4 * g + 4, :],
                                    ALU.mult), key)
                        dve.drain()
                        if n:
                            dve.wait_ge(full.sem, full.at(("og", c, n - 1, j)))
                        v.tensor_reduce(scT[:, j, :], M1.rearrange("p l t -> p t l"), axis=AX.X, op=ALU.add)\
                            .then_inc(sc_ready.sem, sc_ready.did((c, n, j)))
                        dve.drain()
                    for j in range(2):
                        key = ("st", c, n, j)
                        ps = filled(dve, key)
                        done(STT(state[:, h, :], state[:, h, :], E[:, 0, j * P + P - 1:j * P + P], ps[:, 0:DV], ALU.mult, ALU.add), key)
                        dve.drain()
                    if n + 1 < NG:
                        dve.wait_ge(k_ready.sem, k_ready.at((c, n)))
                        differences(n + 1)
                if c == 0:
                    sample_gla_dve(dve)
                else:
                    dve.sem_inc(outs.sem, outs.did("state"))
                dve.wait_ge(ssO.sem, ssO.at(c))
                v.reciprocal(rsO[:, :, :], rsO[:, :, :])
                dve.drain()
                for u in range(4):
                    for p0, n, R in pair_jobs(c):
                        key = ("rb", c, u, p0)
                        ps = filled(dve, key)
                        dve.wait_ge(sig_ready.sem, sig_ready.at(key))
                        for i in range(n):
                            x = vog[0:R, p0 + i, u * UC:(u + 1) * UC]
                            last = STT(x, x, rsO[0:R, p0 + i, u:u + 1], ps[0:R, i * UC:(i + 1) * UC], ALU.mult, ALU.mult)
                        done(last, key)
                        dve.drain()
                        dve.sem_inc(rb_mul.sem, rb_mul.did(key))
                for u in range(4):
                    for p0, n, R in pair_jobs(c):
                        key = ("wo", c, u, p0)
                        ps = filled(dve, key)
                        x = xh[0:R, p0:p0 + n, u * UC:(u + 1) * UC]
                        done(TT(x, ps[0:R, 0:n * UC].rearrange("p (i c) -> p i c", i=n), x, ALU.add), key)
                dve.drain()
                dve.sem_inc(h_ready.sem, h_ready.did(c))
                dve.wait_ge(ss1.sem, ss1.at((c, 1)))
                dve.wait_ge(d_g2[c], 16)
                v.reciprocal(rs1[:, :], rs1[:, :])
                dve.drain()
                for t, R in tiles_of(c):
                    STT(oa[0:R, t, :], xh[0:R, t, :], rs1[0:R, t:t + 1], g2b[0:R, :], ALU.mult, ALU.mult)\
                        .then_inc(n2_ready.sem, n2_ready.did((c, t)))
                dve.drain()
                dve.sem_inc(n2_all.sem, n2_all.did(c))

                def best(ps, n, R, t0, q, key):
                    src = lambda t: ps[0:R, t * P:(t + 1) * P]
                    at = lambda buf, t, lo: (buf[0:R, t0, q + t, lo:lo + 8] if t0 == ST else buf[0:R, t, q, lo:lo + 8])
                    for t in range(n):
                        v.max(at(val, t, 0), src(t))
                    dve.drain()
                    for t in range(n):
                        v.max_index(at(idx, t, 0), at(val, t, 0), src(t))
                        last = v.match_replace(tmp[0:R, t, :], at(val, t, 0), src(t), -3.0e38)
                    done(last, key)
                    dve.drain()
                    for t in range(n):
                        v.max(at(val, t, 8), tmp[0:R, t, :])
                    dve.drain()
                    for t in range(n):
                        v.max_index(at(idx, t, 8), at(val, t, 8), tmp[0:R, t, :])
                    dve.drain()

                for q in range(HC):
                    key = ("s", c, q)
                    if c == 0 and q == HC - 1:
                        pass
                    best(filled(dve, key), TC, P, 0, q, key)
                if c == 0:
                    dve.wait_ge(acc_full.sem, acc_full.at(("qS",)))
                    v.tensor_copy(qSs[:, :, :], bank[6][:, 0:HC * NS].rearrange("p (q b) -> p q b", q=HC)).then_inc(qS_ready, 1)
                    for g in range(4):
                        key = ("sR", g)
                        best(filled(dve, key), 4, NS, ST, 4 * g, key)
            dve.wait_ge(d_scr[CHUNKS - 1], 32)
            route(dve, CHUNKS - 1)
            experts_dve(dve)

OUTS = {"yp": (SEQ, D), "ys": (NS, D), "kp": (W, KVH * HD), "vp": (W, KVH * HD), "sp": (HB, DK, DV),
        "ks": (NS, W, KVH * HD), "vs": (NS, W, KVH * HD), "ss": (NS, HB, DK, DV)}


def unit_columns():
    q = np.arange(HA * HD).reshape(2, 2, 4, HD).transpose(0, 2, 1, 3).ravel()
    at = HA * HD
    cols = {"k": np.arange(at, at + KVH * HD)}
    at += KVH * HD
    cols["va"] = np.arange(at, at + KVH * HD)
    at += KVH * HD
    for name, n in (("qb", HB * DK), ("kb", HB * DK), ("vb", HB * DV), ("rb", HB * DV), ("z", RANK), ("ga", D), ("gb", D)):
        cols[name] = np.arange(at, at + n)
        at += n
    cols["fm"] = np.concatenate([q, cols["k"], cols["qb"], cols["kb"]])
    return cols


def kernel(**inputs):
    import concourse.bacc as bacc
    from concourse.bass_utils import run_bass_kernel_spmd

    x = {k: np.asarray(v) for k, v in inputs.items()}
    f = np.ascontiguousarray
    w_in, w_out, wq = x["w_in"][0], x["w_out"][0], x["peer_wq"][0]
    cols = unit_columns()
    units = []
    for kind, u in UNITS:
        w = w_out if kind == "wo" else wq if kind == "wq" else w_in[:, cols[kind]]
        units.append(w[:, u * UC:(u + 1) * UC].reshape(KC, P, UC).transpose(1, 0, 2).reshape(P, KC * UC))
    kc = x["cache_k_win"][0].reshape(NS, W, KVH * HD)
    vc = x["cache_v_win"][0].reshape(NS, W, KVH * HD)
    arrays = {
        "xp": f(x["x_prompt"][0]), "xs": f(x["x_sample"][:, 0]), "cst": constants(), "w": f(np.stack(units)),
        "g1c": f(x["norm1_g"][0].reshape(KC, P).T), "wz": f(w_in[:, cols["z"]].reshape(KC, P, RANK).transpose(1, 0, 2)),
        "wg": f(x["w_gla_gate"][0]), "bg": f(x["b_gla_gate"][0].reshape(HB, DK).T), "sinks": f(x["attn_sinks"][0]),
        "sinksP": f(np.tile(x["attn_sinks"][0], NS)[:, None]), "g2": f(x["norm2_g"][0]), "glag": f(x["gla_norm_g"][0]),
        "gf": f(x["final_norm_g"]), "kc": f(kc), "vc": f(vc),
        "kTs": f(kc[:, 1:].reshape(NS, W - 1, 2, P).transpose(3, 2, 0, 1)),
        "keysT": f(x["peer_subkeys"][0].reshape(HC, NK, P).transpose(2, 0, 1)),
        "s0": f(x["state_gla"][0]), "u": f(x["peer_u"][0]), "v": f(x["peer_v"][0]),
    }
    nc = bacc.Bacc("TRN2", target_bir_lowering=False, num_devices=1)
    dt = mybir.dt.float32
    a = {k: nc.dram_tensor(f"in_{k}", v.shape, dt, kind="ExternalInput").ap() for k, v in arrays.items()}
    o = {k: nc.dram_tensor(f"out_{k}", s, dt, kind="ExternalOutput").ap() for k, s in OUTS.items()}
    for k in ("h", "n2"):
        o[k] = nc.dram_tensor(f"scratch_{k}", (SEQ + NS, D), dt, kind="Internal").ap()
    build(nc, a, o)
    r = run_bass_kernel_spmd(nc, [{f"in_{k}": v for k, v in arrays.items()}], core_ids=[0]).results[0]
    r = {k: r[f"out_{k}"] for k in OUTS}
    kv = (1, -1, W, KVH, HD)
    return (r["yp"].reshape(1, SEQ, D), r["ys"].reshape(NS, 1, D), r["kp"].reshape(kv), r["vp"].reshape(kv),
            r["sp"].reshape(1, 1, HB, DK, DV), r["ks"].reshape(kv), r["vs"].reshape(kv), r["ss"].reshape(1, NS, HB, DK, DV))
```

```python
import itertools
import numpy as np
import concourse.bass as bass
from concourse import mybir
from contextlib import ExitStack

P = 128
D = 1024
KC = D // P
SEQ = 1024
NS = 8
TILES = SEQ // P
CHUNKS = 2
TC = TILES // CHUNKS
CT = TC * P
ST = TC
HA, KVH, HD, W = 16, 4, 64, 128
HB, DK, DV = 4, 128, 256
RANK = 16
GATE_TEMP = 16.0
EPS = 1e-6
PH, NK, TOPK = 8, 128, 16
NE = NK * NK
PAIRS = PH * TOPK
NEAR = 4
CANDS = NEAR * TOPK + (TOPK - NEAR) * NEAR
HC = 2 * PH
UC = 256
LV = 7
NEG = -1.0e30

UNITS = ([("fm", i) for i in range(9)] + [("va", 0)] + [("vb", i) for i in range(4)]
         + [("ga", i) for i in range(4)] + [("rb", i) for i in range(4)] + [("gb", i) for i in range(4)]
         + [("wo", i) for i in range(4)] + [("wq", i) for i in range(8)])
NU = len(UNITS)
WR = 2
FMB = 19
SLOTS = 16
GROUPS = PAIRS // SLOTS
USES = TC * GROUPS
ROUTE_GAPS = (TC - 1) * 9 + TC
N_OUT = 3 + 1 + 2 + 1

EARLY = ([(("route", i), 2) for i in range(ROUTE_GAPS)]
         + [x for n in range(4 * TC + 2)
            for x in ([(("scores", n, i), 1) for i in range(4)] if n < 4 * TC else [])
            + ([(("values", n - 2, i), 2) for i in range(2)] if n >= 2 else [])]
         + [(("gla", n, i), (4, 1, 2, 1, 2, 1, 2, 1)[i]) for n in range(2 * HB) for i in range(8)]
         + [(("norm", 0), 8)] + [(("rb", i), 4) for i in range(8)] + [(("gb", i), 4) for i in range(8)]
         + [(("merged", 0), 8)] + [(("wo", i), 4) for i in range(6)] + [(("n2", 0), 4), (("n2", 1), 8)] + [(("best", q), 4) for q in range(HC)])

C_ID, C_DIST, C_RESET, C_MASK = 0, 128, 384, 512
C_IOTA = C_MASK + 8 * 128
C_DIST_S = C_IOTA + 16
C_SLOPE_S = C_DIST_S + 128
C_END = C_SLOPE_S + 1


def slopes():
    return [2.0 ** (-8.0 * (h + 1) / HA) for h in range(HA)]


def constants():
    c = np.zeros((P, C_END), np.float32)
    i = np.arange(P)
    c[:, C_ID:C_ID + P] = np.eye(P)
    dist = i[:, None] + P - np.arange(2 * P)[None, :]
    c[:, C_DIST:C_DIST + 2 * P] = np.where((dist >= 0) & (dist < W), -dist, NEG)
    c[:, C_RESET:C_RESET + P] = 1.0
    for l in range(LV):
        m = (P // 2) >> l
        s, t = i[:, None], i[None, :]
        c[:, C_MASK + l * P:C_MASK + (l + 1) * P] = (t // (2 * m) == s // (2 * m)) & (t % (2 * m) >= m) & (s % (2 * m) < m)
    c[:, C_MASK + LV * P:C_MASK + (LV + 1) * P] = np.eye(P)
    c[:, C_IOTA:C_IOTA + 16] = np.arange(16)
    c[:, C_DIST_S:C_DIST_S + P] = -(P - 1 - i)[None, :]
    c[:, C_SLOPE_S] = np.array(slopes())[i % HA]
    return c


class Signal:

    def __init__(self, sem, keys):
        self.sem, self.keys, self.n = sem, {k: i + 1 for i, k in enumerate(keys)}, 0

    def at(self, key):
        return self.keys[key]

    def did(self, key):
        self.n += 1
        assert self.keys[key] == self.n, (key, self.keys[key], self.n)
        return 1


def tiles_of(c):
    return [(t, P) for t in range(TC)] + ([(ST, NS)] if c == 0 else [])


def pair_jobs(c):
    return [(0, 2, P), (2, 2, P)] + ([(ST, 1, NS)] if c == 0 else [])


def psum_jobs():
    jobs = []
    for c in range(CHUNKS):
        for t, _ in tiles_of(c):
            jobs += [(("nT", c, t, g), "dve") for g in range(2)]
        for b in range(FMB):
            jobs.append((("fm", c, b), "act"))
        tm = lambda kind, u, eng: [((kind, c, u, p[0]), eng) for p in pair_jobs(c)]
        jobs += tm("va", 0, "act")
        for n in range(HA // 4 * TC + 2):
            if n < 4 * TC:
                if n % 4 == 0:
                    jobs += tm("vb", n // 4, "act")
                jobs += [(("S", c, n, g), "dve") for g in range(2)]
            if 1 <= n <= 4 * TC:
                jobs += [(("PT", c, n - 1, g), "act") for g in range(2)]
            if n >= 2:
                jobs.append((("O", c, n - 2), "dve"))
        if c == 0:
            jobs += [(("sS",), "dve"), (("sST",), "dve"), (("sPT",), "dve"), (("sO",), "dve"),
                     (("sOt", 0), "dve"), (("sOt", 1), "dve")]
        if c == CHUNKS - 1:
            jobs.append((("kwin",), "dve"))
        jobs += [(("gate", c, h), "dve") for h in range(HB)]
        if c == 0:
            jobs.append((("gateS",), "dve"))
        for n in range(2 * HB):
            for j in range(2):
                jobs += [(("L", c, n, j, g), "dve") for g in range(2)]
            jobs += [(("kdT", c, n), "act")]
            for j in range(2):
                jobs += [(("og", c, n, j), "act"), (("st", c, n, j), "dve")]
            for p in pair_jobs(c):
                if (p[0] != 0) == n % 2:
                    jobs.append((("ga", c, n // 2, p[0]), "act"))
        if c == 0:
            jobs.append((("kSt",), "dve"))
            for b in range(NS):
                jobs += [(("vB", b, g), "dve") for g in range(2)]
        for kind, eng in (("rb", "dve"), ("gb", "act")):
            for u in range(4):
                jobs += tm(kind, u, eng)
        for t, _ in tiles_of(c):
            jobs += [(("uT", c, t, g), "act") for g in range(2)]
        for u in range(4):
            jobs += tm("wo", u, "dve")
        for t, _ in tiles_of(c):
            jobs += [(("n2T", c, t, g), "act") for g in range(2)]
        for q in range(HC + 1):
            jobs += [(("q", c, q), "act")] if q < HC else []
            jobs += [(("s", c, q - 1), "dve")] if q >= 1 else []
        if c == 0:
            jobs += [(("sR", g), "dve") for g in range(4)]
    return jobs


def sample_accumulations():
    return [("fmS",), ("ogS",), ("qS",)]


def build(nc, a, o):
    fp32, u32, bf16 = mybir.dt.float32, mybir.dt.uint32, mybir.dt.bfloat16
    ALU, ACT, AX = mybir.AluOpType, mybir.ActivationFunctionType, mybir.AxisListType
    SL = slopes()

    ctx = ExitStack()
    with ctx:
        def sb(name, shape, dt=fp32):
            return ctx.enter_context(nc.sbuf_tensor(name, shape, dt))

        def sem(name):
            return ctx.enter_context(nc.semaphore(name))

        cst = sb("cst", [P, C_END])
        big = sb("big", [P, SLOTS * D])
        nTb = sb("nTb", [P, KC * CT])
        arena = sb("arena", [P, 25 * 256])
        kaT = sb("kaT", [P, 2, P + CT])
        va = sb("va", [P, 1 + TC, KVH * HD])
        qbT = sb("qbT", [P, HB, CT])
        kbT = sb("kbT", [P, HB, CT])
        bTb = sb("bTb", [P, HB * CT])
        wring = sb("wring", [P, WR, KC, UC])
        Pbb = sb("Pbb", [P, 2 * 4 * 256])
        glag = sb("glag", [P, DV])
        state = sb("state", [P, HB, DV])
        scT = sb("scT", [P, 2, P])
        E0b = sb("E0b", [P, 256])
        kdTok = sb("kdTok", [P, 2, P])
        val = sb("val", [P, 1 + TC, HC, TOPK])
        idx = sb("idx", [P, 1 + TC, HC, TOPK], u32)
        picks = sb("picks", [P, 2, TILES, PAIRS])
        early_dots = sb("early_dots", [P, TC * PAIRS])
        gateS = sb("gateS", [NS, PAIRS])
        eidS = sb("eidS", [NS, PAIRS])
        g1c = sb("g1c", [P, KC])
        wz = sb("wz", [P, KC, RANK])
        zbT = sb("zbT", [RANK, CT])
        wg = sb("wg", [RANK, HB * DK])
        bg = sb("bg", [P, HB])
        nsink = sb("nsink", [P, HA])
        nsinkP = sb("nsinkP", [P, 1])
        nTs = sb("nTs", [P, KC, NS])
        fmS = sb("fmS", [P, FMB, NS])
        qz = sb("qz", [P, HB, NS, NS])
        st1 = sb("st1", [P, 1 + TC])
        rs1 = sb("rs1", [P, 1 + TC])
        stO = sb("stO", [P, 1 + TC, HB])
        rsO = sb("rsO", [P, 1 + TC, HB])
        mx = sb("mx", [P, 4, 4])
        nm = sb("nm", [P, 4, 4])
        sk = sb("sk", [P, 4, 4])
        rsum = sb("rsum", [P, 4, 4])
        esink = sb("esink", [P, 4, 4])
        rden = sb("rden", [P, 4, 4])
        smS = sb("smS", [P, 6])
        epst = sb("epst", [P, 1])
        yS = sb("yS", [P, HB, NS])
        tS = sb("tS", [P, HB, NS])
        aS = sb("aS", [P, HB, NS])
        zS = sb("zS", [P, NS])
        qSs = sb("qSs", [P, HC, NS])
        oS = sb("oS", [HD, P])
        gs = sb("gs", [P, PH])

        eidx, gate = picks[:, 0].bitcast(u32), picks[:, 1]
        n2e = picks[:, :, TC:, :].rearrange("p a t k -> p a (t k)")
        vaS, kSn = early_dots[0:NS, 0:KVH * HD], early_dots[0:NS, KVH * HD:2 * KVH * HD]
        ident = cst[:, C_ID:C_ID + P]
        dist = cst[:, C_DIST:C_DIST + 2 * P]
        ones = cst[:, C_RESET:C_RESET + P]
        masks = cst[:, C_MASK:C_MASK + 8 * P].rearrange("p (l t) -> p l t", l=8)
        iota = cst[:, C_IOTA:C_IOTA + TOPK]
        distS = cst[:, C_DIST_S:C_DIST_S + P]
        slopeS = cst[:, C_SLOPE_S:C_SLOPE_S + 1]
        xh = big[:, 0:5 * D].rearrange("p (t d) -> p t d", t=5)
        oa = big[:, 5 * D:10 * D].rearrange("p (t d) -> p t d", t=5)
        vog = big[:, 10 * D:15 * D].rearrange("p (t d) -> p t d", t=5)
        s0 = [big[:, 15 * D:16 * D].rearrange("p (h d) -> p h d", h=HB),
              Pbb[:, 0:D].rearrange("p (h d) -> p h d", h=HB)]
        nT = nTb[:, :].rearrange("p (k t) -> p k t", k=KC)
        qaT = arena[:, 0:8 * CT].rearrange("p (b t) -> p b t", b=8)
        PT = arena[:, 4096:6144].rearrange("p (n g c) -> p n g c", n=2, g=2)
        Y = arena[:, 0:HB * CT].rearrange("p (h t) -> p h t", h=HB)
        Tt = arena[:, HB * CT:2 * HB * CT].rearrange("p (h t) -> p h t", h=HB)
        E = arena[:, 0:8 * 256].rearrange("p (l t) -> p l t", l=8)
        E0 = [arena[:, 8 * 256:9 * 256], E0b[:, :]]
        Qd = arena[:, 9 * 256:17 * 256].rearrange("p (l t) -> p l t", l=8)
        Kd = arena[:, 17 * 256:25 * 256].rearrange("p (l t) -> p l t", l=8)
        junkO = arena[:, 0:5 * D].rearrange("p (t h d) -> p t h d", t=5, h=HB)
        qh = arena[:, 5 * D:5 * D + 2 * CT].rearrange("p (n t) -> p n t", n=2)
        tmp = arena[:, 0:CT].rearrange("p (t n) -> p t n", t=TC)
        bT = bTb[:, :].rearrange("p (h t) -> p h t", h=HB)
        kTs = bTb[:, :].rearrange("p (q b s) -> p q b s", q=2, b=NS)
        keysT = bTb[:, :].rearrange("p (q n) -> p q n", q=HC)
        Pb = Pbb[:, :].rearrange("p (n i s) -> p n i s", n=2, i=4)
        vS = Pbb[:, :].rearrange("p (b c) -> p b c", b=NS)
        M1 = Pbb[:, 0:D].rearrange("p (l t) -> p l t", l=8)
        sig = Pbb[:, D:2 * D].rearrange("p (n i c) -> p n i c", n=2, i=2)
        by_head = lambda x: x.rearrange("p (h k) -> p h k", h=PH)
        flat = lambda x: x.rearrange("p a d -> p (a d)")
        route_bufs = [(by_head(flat(oa[:, 0:2, :])), by_head(flat(oa[:, 2:4, :])), flat(vog[:, 0:2, :])),
                      (by_head(flat(kbT[:, :, :])), by_head(flat(qbT[:, :, :])), flat(wring[:, 0, :, :]))]
        onehot = Pbb[:, :].rearrange("p (h k j) -> p h k j", h=PH, k=TOPK)
        g2b = Pbb[:, D:2 * D]
        kwin = qz[:, :, :, :].rearrange("p h a b -> p (h a b)")
        SsT, Ps, PsT = (arena[:, 4096 + i * P:4096 + (i + 1) * P] for i in range(3))

        bank = [ctx.enter_context(nc.psum_tensor(f"bank{i}", [P, 512], fp32)) for i in range(8)]
        RING = 6
        jobs = psum_jobs()
        full = Signal(sem("full"), [k for k, _ in jobs])
        evac = {e: Signal(sem(f"evac_{e}"), [k for k, who in jobs if who == e]) for e in ("act", "dve")}
        owner = dict(jobs)
        number = {k: i for i, (k, _) in enumerate(jobs)}
        acc_full = Signal(sem("acc_full"), [("fmS",), ("qS",)])
        acc_free = Signal(sem("acc_free"), sample_accumulations())

        def B(key):
            return bank[number[key] % RING]

        def room(pe, key):
            n = number[key] - RING
            if n >= 0:
                before = jobs[n][0]
                pe.wait_ge(evac[owner[before]].sem, evac[owner[before]].at(before))
            return B(key)

        def emptied(eng, key):
            eng.wait_ge(evac[owner[key]].sem, evac[owner[key]].at(key))

        def filled(eng, key):
            eng.wait_ge(full.sem, full.at(key))
            return B(key)

        CC = range(CHUNKS)
        both = [(c, t) for c in CC for t, _ in tiles_of(c)]
        NQ = 4 * TC
        d_cst, d_par = sem("d_cst"), sem("d_par")
        d_x = [sem(f"d_x{c}") for c in CC]
        d_w = [sem(f"d_w{i}") for i in range(WR)]
        d_kv = sem("d_kv")
        d_vS = sem("d_vS")
        d_s0 = [sem(f"d_s0{i}") for i in range(2)]
        d_keys = [sem(f"d_keys{c}") for c in CC]
        d_g2 = [sem(f"d_g2{c}") for c in CC]
        d_scr = [sem(f"d_scr{c}") for c in CC]
        d_out = sem("d_out")
        d_st = [sem(f"d_st{i}") for i in range(2)]
        init = sem("init")
        ss1 = Signal(sem("ss1"), [(c, i) for c in CC for i in range(2)])
        n_tok = Signal(sem("n_tok"), both)
        nm_ready = Signal(sem("nm_ready"), [(c, n) for c in CC for n in range(NQ)])
        p_ready = Signal(sem("p_ready"), [(c, n) for c in CC for n in range(NQ)])
        smx = Signal(sem("smx"), ["nm", "p"])
        smp = Signal(sem("smp"), ["p"])
        y_ready = Signal(sem("y_ready"), [*CC])
        t_ready = Signal(sem("t_ready"), [*CC])
        aS_in = sem("aS_in")
        aS_out = sem("aS_out")
        NG = 2 * HB
        gk = [(c, n) for c in CC for n in range(NG)]
        d_ready = Signal(sem("d_ready"), gk)
        e_ready = Signal(sem("e_ready"), gk)
        q_ready = Signal(sem("q_ready"), gk)
        k_ready = Signal(sem("k_ready"), gk)
        sc_ready = Signal(sem("sc_ready"), [(c, n, j) for c, n in gk for j in range(2)])
        s0a = Signal(sem("s0a"), range(NS))
        s0n = Signal(sem("s0n"), range(NS))
        ogb = Signal(sem("ogb"), range(NS))
        fmz = sem("fmz")
        knew = sem("knew")
        gates_k = [(k, c, u, p[0]) for c in CC for k in ("ga", "rb", "gb") for u in range(4) for p in pair_jobs(c)]
        sig_ready = Signal(sem("sig_ready"), gates_k)
        sig_used = Signal(sem("sig_used"), gates_k)
        rb_mul = Signal(sem("rb_mul"), [k for k in gates_k if k[0] == "rb"])
        gl_mul = Signal(sem("gl_mul"), [k for k in gates_k if k[0] == "rb"])
        u_ready = Signal(sem("u_ready"), [*CC])
        ssO = Signal(sem("ssO"), [*CC])
        rstdO = Signal(sem("rstdO"), [*CC])
        h_ready = Signal(sem("h_ready"), [*CC])
        n2_ready = Signal(sem("n2_ready"), both)
        n2_all = Signal(sem("n2_all"), [*CC])
        qS_ready = sem("qS_ready")
        sv_ready = Signal(sem("sv_ready"), [*CC])
        ex_ready = Signal(sem("ex_ready"), [*CC])
        picked = Signal(sem("picked"), [x for x in both if x[0] == 0 and x[1] != ST] + [(1, 0), (0, ST), (1, 1), (1, 2), (1, 3)])
        routed = Signal(sem("routed"), [*CC])
        outs = Signal(sem("outs"), ["kSn", "kwin", "state"])
        gate_used = {k: i for i, k in enumerate(gates_k)}

        def unit_end(c, i):
            kind, u = UNITS[i]
            if kind in ("fm", "wq"):
                return ("fm" if kind == "fm" else "q", c, 2 * u + 1)
            return (kind, c, u, pair_jobs(c)[-1][0])



        ring = [big[:, r * D:(r + 1) * D] for r in range(SLOTS)]
        n2t, ht = nTb[:, 0:D], nTb[:, D:2 * D]
        acc = [nTb[:, 2 * D:3 * D], nTb[:, 3 * D:4 * D]]
        diag = [arena[:, k * P:(k + 1) * P] for k in range(SLOTS // 2)]
        gfb = arena[:, D:2 * D]
        dots, act_g, wgt = (arena[:, 2 * D + i * P:2 * D + (i + 1) * P] for i in range(3))
        ysum = arena[:, 3 * D:4 * D]
        ysq = arena[:, 4 * D:5 * D]
        yout = arena[:, 5 * D:6 * D]
        ix = sb("ix", [P, 2, SLOTS], u32)
        dg = sb("dg", [P, SLOTS])
        zero = arena[:, 2 * D + 3 * P:2 * D + 5 * P].bitcast(bf16)
        ixS = sb("ixS", [P, NS], u32)
        gT = sb("gT", [P, NS])
        dS = sb("dS", [P, NS, 2])
        aT = sb("aT", [P, NS])
        wzS = sb("wzS", [P, NS, NS])
        fs = sb("fs", [P, 2])
        eidx_f = eidx.rearrange("p t k -> p (t k)")
        gate_f = gate.rearrange("p t k -> p (t k)")

        eslots = [ring[k].rearrange("p (a d) -> p a d", a=2) for k in (4, 9, 14, 15)]
        ES = len(eslots)
        early_in = [sem(f"early_in{r}") for r in range(ES)]
        early_used = [sem(f"early_used{r}") for r in range(ES)]
        d_n2e = sem("d_n2e")
        early_at, early_rows = {}, 0
        for point, rows in EARLY:
            early_at[point] = early_rows
            early_rows += rows
        assert early_rows <= TC * PAIRS
        gathered = [sem(f"gathered{r}") for r in range(SLOTS)]
        slot_used = [sem(f"slot_used{r}") for r in range(SLOTS)]
        d_n2, d_h, d_gf, d_y = sem("d_n2"), sem("d_h"), sem("d_gf"), sem("d_y")
        n2_used, h_used = sem("n2_used"), sem("h_used")
        dots_ready, act_ready, wgt_ready = sem("dots_ready"), sem("act_ready"), sem("wgt_ready")
        diag_ready = sem("diag_ready")
        ix_ready = sem("ix_ready")
        v_done, v_free = sem("v_done"), sem("v_free")
        y_sum, y_rms, y_out, y_free = sem("y_sum"), sem("y_rms"), sem("y_out"), sem("y_free")
        sx = {k: sem("sx_" + k) for k in ("T", "ix", "n2b", "dot", "gelu", "w", "v", "y", "rms", "out")}

        passed = {e: sem(f"passed_{e}") for e in ("pool", "act", "dve", "pe")}

        def hold(eng, name, s, value):
            eng.wait_ge(s, value)
            eng.sem_inc(passed[name], 1)

        def use(first, tile, phase, i, b):
            if first == 0:
                return tile * GROUPS + b + i * 2
            return tile * (2 * GROUPS) + (USES + 1 + phase * GROUPS + b) + i * 2

        def experts_pool(pool):
            pool.wait_ge(d_scr[CHUNKS - 1], 32)
            pool.wait_ge(full.sem, full.at(("n2T", CHUNKS - 1, TC - 1, 1)))
            for r in range(ES):
                pool.wait_ge(early_used[r], TC * PAIRS // ES)
            for r in range(SLOTS):
                pool.sem_inc(slot_used[r], 1)
            for first in (0, TC):
                if first:
                    pool.wait_ge(sx["ix"], 1)
                    for r in range(SLOTS):
                        pool.wait_ge(slot_used[r], USES + 1)
                        table = a["u"] if r < NS else a["v"]
                        pool.indirect_dma_start(out=ring[r], out_offset=None, in_=table,
                                                in_offset=bass.IndirectOffsetOnAxis(ap=ixS[:, r % NS:r % NS + 1], axis=0))\
                            .then_inc(gathered[r], 16)
                    pool.wait_ge(picked.sem, picked.at((CHUNKS - 1, TC - 1)))
                with pool.Fori(0, TC) as tile:
                    for phase in ((1,) if first == 0 else (0, 1)):
                        table = a["u"] if phase == 0 else a["v"]
                        with pool.Fori(0, GROUPS // 2) as i:
                            for b in range(2):
                                k = tile * PAIRS + i * (2 * SLOTS) + (first * PAIRS + b * SLOTS)
                                nc.gpsimd.tensor_copy(ix[:, b, :], eidx_f[:, bass.ds(k, SLOTS)]).then_inc(ix_ready, 1)
                                hold(pool, "pool", ix_ready, use(first, tile, phase, i, b) + (0 if first else 1))
                                for r in range(SLOTS):
                                    hold(pool, "pool", slot_used[r], use(first, tile, phase, i, b) + 1)
                                    pool.indirect_dma_start(out=ring[r], out_offset=None, in_=table,
                                                            in_offset=bass.IndirectOffsetOnAxis(ap=ix[:, b, r:r + 1], axis=0))\
                                        .then_inc(gathered[r], 16)
            pool.wait_ge(d_out, 16 * N_OUT)
            for i in range(2):
                pool.wait_ge(d_st[i], 16 * (NS // 2))

        def experts_sp(sp):
            sp.wait_ge(evac["dve"].sem, evac["dve"].at(("s", CHUNKS - 1, HC - 1)))
            for c in CC:
                sp.wait_ge(d_scr[c], 64 if c == 0 else 32)
            sp.dma_start(gfb, a["gf"].partition_broadcast(P)).then_inc(d_gf, 16)
            for first in (0, TC):
                done = 1 if first else 0
                if first:
                    sp.wait_ge(h_used, TC + 1)
                    sp.dma_start(ht[0:NS, :], o["h"][SEQ:SEQ + NS, :]).then_inc(d_h, 16)
                    sp.wait_ge(sx["out"], 1)
                    sp.dma_start(o["ys"], yout[0:NS, :]).then_inc(d_y, 16)
                    sp.wait_ge(d_y, 16 * (TC + 1))
                    sp.sem_inc(y_free, 1)
                else:
                    sp.dma_start(n2t[0:NS, :], o["n2"][SEQ:SEQ + NS, :]).then_inc(d_n2, 16)
                with sp.Fori(0, TC) as tile:
                    if first:
                        sp.wait_ge(n2_used, tile + 1)
                        sp.dma_start(n2t, o["n2"][bass.ds((tile + first) * P, P), :]).then_inc(d_n2, 16)
                    sp.wait_ge(h_used, tile + (first + done + 1))
                    sp.dma_start(ht, o["h"][bass.ds((tile + first) * P, P), :]).then_inc(d_h, 16)
                    sp.wait_ge(y_out, tile + (first + 1))
                    sp.dma_start(o["yp"][bass.ds((tile + first) * P, P), :], yout).then_inc(d_y, 16)
                    sp.wait_ge(d_y, tile * 16 + (16 * (first + done) + 16))
                    sp.sem_inc(y_free, 1)

        def experts_dve(dve):
            v = nc.vector
            TT, STT = v.tensor_tensor, v.scalar_tensor_tensor
            v.memset(zero[:, :], 0.0)
            v.memset(wzS[:, :, :], 0.0)
            dve.drain()
            dve.sem_inc(v_free, 1)
            dve.sem_inc(h_used, 1)
            dve.wait_ge(d_gf, 16)

            def products(tile):
                with dve.Fori(0, GROUPS // 2) as i:
                    for b in range(2):
                        for r in range(SLOTS):
                            dve.wait_ge(gathered[r], use(TC, tile, 0, i, b) * 16 + 16)
                            v.tensor_tensor_reduce(out=ring[r], in0=ring[r], in1=n2t, scale=1.0, scalar=0.0, op0=ALU.mult, op1=ALU.add,
                                                   accum_out=dg[:, r:r + 1]).then_inc(slot_used[r], 1)
                        dve.drain()
                        v.tensor_copy(dots[:, bass.ds(i * (2 * SLOTS) + b * SLOTS, SLOTS)], dg[:, :])
                        dve.drain()
                dve.sem_inc(n2_used, 1)

            def sums(first, tile):
                dve.sem_inc(dots_ready, 1)
                v.memset(acc[0], 0.0)
                v.memset(acc[1], 0.0)
                dve.drain()
                dve.wait_ge(act_ready, tile + (first + 1))
                k = (tile + first) * PAIRS
                TT(wgt, act_g, gate_f[:, k:k + PAIRS] if first == 0 else gate_f[:, bass.ds(k, PAIRS)], ALU.mult).then_inc(wgt_ready, 1)
                dve.drain()
                def odd_slots(before, w):
                    for r in range(1, SLOTS, 2):
                        s = acc[(r // 2) % 2]
                        dve.wait_ge(slot_used[(r - 4) % SLOTS], before + (2 if r >= 4 else 1))
                        dve.wait_ge(gathered[r], before * 16 + 16)
                        STT(s, ring[r], w(r), s, ALU.mult, ALU.add).then_inc(slot_used[r], 1)

                if first == 0:
                    gap = itertools.count()
                    every = 2 if tile == 0 else 1

                    def group():
                        j, rest = divmod(next(gap), every)
                        if rest == 0 and j < GROUPS:
                            odd_slots(tile * GROUPS + j, lambda r: wgt[:, j * SLOTS + r:j * SLOTS + r + 1])

                    route_tile(dve, CHUNKS - 1, tile, P, route_bufs[1], group)
                    if tile == 0:
                        route_tile(dve, 0, ST, NS, route_bufs[1], group)
                else:
                    with dve.Fori(0, GROUPS // 2) as i:
                        for b in range(2):
                            odd_slots(use(first, tile, 1, i, b), lambda r: wgt[:, bass.ds(i * (2 * SLOTS) + (b * SLOTS + r), 1)])
                dve.drain()
                TT(ysum, acc[0], acc[1], ALU.add)
                dve.drain()
                done = 1 if first else 0
                dve.wait_ge(d_h, tile * 16 + (16 * (first + done) + 16))
                TT(ysum, ysum, ht, ALU.add)
                dve.drain()
                dve.sem_inc(h_used, 1)
                dve.wait_ge(v_done, tile + (first + 1))
                for g in range(2):
                    TT(ysum[:, g * 512:(g + 1) * 512], bank[6 + g][:, :], ysum[:, g * 512:(g + 1) * 512], ALU.add)
                dve.drain()
                dve.sem_inc(v_free, 1)
                dve.sem_inc(y_sum, 1)
                dve.wait_ge(y_rms, tile + (first + 1))
                v.reciprocal(fs[:, 1:2], fs[:, 1:2])
                dve.drain()
                dve.wait_ge(y_free, tile + (first + done + 1))
                STT(yout, ysum, fs[:, 1:2], gfb, ALU.mult, ALU.mult).then_inc(y_out, 1)
                dve.drain()

            for t in range(TC):
                if t == 1:
                    dve.wait_ge(sx["T"], 1)
                    v.tensor_copy(ixS[:, :], bank[0][:, 0:NS]).then_inc(sx["ix"], 1)
                v.tensor_copy(dots, early_dots[:, t * PAIRS:(t + 1) * PAIRS])
                dve.drain()
                sums(0, t)
            gates(dve, CHUNKS - 1)
            dve.wait_ge(sx["T"], 2)
            v.tensor_copy(gT[:, :], bank[0][:, NS:2 * NS])
            for t in range(NS):
                if t:
                    dve.wait_ge(sx["dot"], 2 * t)
                    dve.sem_inc(slot_used[t - 1], 1)
                dve.wait_ge(gathered[t], USES * 16 + 16)
                for g in range(2):
                    n = 2 * t + g
                    dve.wait_ge(sx["n2b"], n + 1)
                    x = ring[t][:, g * 512:(g + 1) * 512]
                    v.tensor_tensor_reduce(out=x, in0=x, in1=bank[1 + n % 4][:, :], scale=1.0, scalar=0.0, op0=ALU.mult, op1=ALU.add,
                                           accum_out=dS[:, t, g:g + 1]).then_inc(sx["dot"], 1)
            dve.wait_ge(sx["dot"], 2 * NS)
            dve.sem_inc(slot_used[NS - 1], 1)
            dve.sem_inc(n2_used, 1)
            dve.drain()
            TT(aT[:, :], dS[:, :, 0], dS[:, :, 1], ALU.add)
            dve.drain()
            dve.sem_inc(sx["dot"], 1)
            dve.wait_ge(sx["gelu"], 1)
            for t in range(NS):
                last = TT(wzS[:, t, t:t + 1], aT[:, t:t + 1], gT[:, t:t + 1], ALU.mult)
            dve.drain()
            dve.sem_inc(sx["w"], 1)
            dve.wait_ge(sx["v"], 1)
            dve.wait_ge(d_h, TC * 16 + 16)
            for g in range(2):
                TT(ysum[0:NS, g * 512:(g + 1) * 512], bank[6 + g][0:NS, :], ht[0:NS, g * 512:(g + 1) * 512], ALU.add)
            dve.drain()
            dve.sem_inc(h_used, 1)
            dve.sem_inc(v_free, 1)
            dve.sem_inc(sx["y"], 1)
            dve.wait_ge(sx["rms"], 1)
            v.reciprocal(fs[0:NS, 1:2], fs[0:NS, 1:2])
            dve.wait_ge(y_free, TC + 1)
            dve.drain()
            STT(yout[0:NS, :], ysum[0:NS, :], fs[0:NS, 1:2], gfb[0:NS, :], ALU.mult, ALU.mult).then_inc(sx["out"], 1)
            dve.drain()
            with dve.Fori(0, TC) as tile:
                hold(dve, "dve", d_n2, tile * 16 + 32)
                products(tile)
                sums(TC, tile)

        def experts_act(act, route_exp):
            A = nc.scalar.activation
            act.sem_inc(y_free, 1)
            for first in (0, TC):
                if first:
                    route_exp(CHUNKS - 1)
                    act.wait_ge(sx["dot"], 2 * NS + 1)
                    A(aT[:, :], aT[:, :], ACT.Gelu).then_inc(sx["gelu"], 1)
                    act.wait_ge(sx["y"], 1)
                    A(ysq[0:NS, :], ysum[0:NS, :], ACT.Square, accum_out=fs[0:NS, 0:1])
                    act.drain()
                    A(fs[0:NS, 1:2], fs[0:NS, 0:1], ACT.Sqrt, scale=1.0 / D, bias=epst[0:NS, 0:1]).then_inc(sx["rms"], 1)
                    act.drain()
                with act.Fori(0, TC) as tile:
                    act.wait_ge(dots_ready, tile + (first + 1))
                    A(act_g, dots, ACT.Gelu).then_inc(act_ready, 1)
                    act.wait_ge(wgt_ready, tile + (first + 1))
                    with act.Fori(0, GROUPS // 2) as i:
                        for b in range(2):
                            for k in range(SLOTS // 2):
                                hold(act, "act", slot_used[2 * k], use(first, tile, 1, i, b) + 1)
                                A(diag[k], ident, ACT.Copy, scale=wgt[:, bass.ds(i * (2 * SLOTS) + (b * SLOTS + 2 * k), 1)])\
                                    .then_inc(diag_ready, 1)
                    act.wait_ge(y_sum, tile + (first + 1))
                    A(ysq, ysum, ACT.Square, accum_out=fs[:, 0:1])
                    act.drain()
                    A(fs[:, 1:2], fs[:, 0:1], ACT.Sqrt, scale=1.0 / D, bias=epst[:, 0:1]).then_inc(y_rms, 1)
                    act.drain()
        def experts_pe(pe):
            mm, tr = nc.tensor.matmul, nc.tensor.transpose
            for first, skip, count in ((0, 0, 1), (0, 1, TC - 1), (TC, 0, TC)):
                if skip:
                    pe.wait_ge(picked.sem, picked.at((0, ST)))
                    emptied(pe, ("s", CHUNKS - 1, HC - 1))
                    tr(bank[0][:, 0:NS], eidS[:, :], ident[0:NS, 0:NS]).then_inc(sx["T"], 1)
                if first:
                    pe.wait_ge(routed.sem, routed.at(CHUNKS - 1))
                    tr(bank[0][:, NS:2 * NS], gateS[:, :], ident[0:NS, 0:NS]).then_inc(sx["T"], 1)
                    pe.wait_ge(d_n2, 16)
                    for t in range(NS):
                        for g in range(2):
                            n = 2 * t + g
                            if n >= 4:
                                pe.wait_ge(sx["dot"], n - 3)
                            mm(bank[1 + n % 4][:, :], ident[0:NS, t:t + 1].broadcast_to((NS, P)), n2t[0:NS, g * 512:(g + 1) * 512],
                               start=True, stop=True).then_inc(sx["n2b"], 1)
                    pe.wait_ge(sx["w"], 1)
                    pe.wait_ge(v_free, TC + 1)
                    for t in range(NS):
                        pe.wait_ge(gathered[NS + t], USES * 16 + 16)
                        for g in range(2):
                            last = mm(bank[6 + g][0:NS, :], wzS[:, t, :], ring[NS + t][:, g * 512:(g + 1) * 512], start=(t == 0), stop=(t == NS - 1))
                        last.then_inc(slot_used[NS + t], 1)
                    pe.drain()
                    pe.sem_inc(sx["v"], 1)
                with pe.Fori(0, count) as tile:
                    pe.wait_ge(v_free, tile + (first + skip + (2 if first else 1)))
                    pe.wait_ge(wgt_ready, tile + (first + skip + 1))
                    for g in range(2):
                        mm(bank[6 + g][:, :], zero[:, 0:P], zero[:, :], start=True, stop=False)
                    with pe.Fori(0, GROUPS // 2) as i:
                        for b in range(2):
                            for k in range(SLOTS // 2):
                                r = 2 * k
                                pe.wait_ge(diag_ready, tile * (PAIRS // 2) + i * SLOTS
                                           + ((first + skip) * (PAIRS // 2) + b * (SLOTS // 2) + k + 1))
                                pe.wait_ge(gathered[r], use(first, tile, 1, i, b) * 16 + (16 + 16 * skip * GROUPS))
                                for g in range(2):
                                    last = mm(bank[6 + g][:, :], diag[k], ring[r][:, g * 512:(g + 1) * 512], start=False, stop=False)
                                last.then_inc(slot_used[r], 1)
                    for g in range(2):
                        last = mm(bank[6 + g][:, :], zero[:, 0:P], zero[:, :], start=False, stop=True)
                    last.then_inc(v_done, 1)
        def scTm(pe, c, n, j):
            pe.wait_ge(sc_ready.sem, sc_ready.at((c, n, j)))
            return scT[:, j, :]

        def sample_attention_pe(pe):
            mm, tr = nc.tensor.matmul, nc.tensor.transpose
            pe.wait_ge(knew, 1)
            ps = room(pe, ("sS",))
            for half in range(2):
                lo = half * 64
                for b in range(NS):
                    for Q in range(2):
                        q = 2 * Q + half
                        last = mm(ps[:, b * HA + q * 4:b * HA + q * 4 + 4], kTs[lo:lo + 64, Q, b, :], fmS[lo:lo + 64, 4 * Q:4 * Q + 4, b],
                                  start=True, stop=True)
                if half == 0:
                    pe.drain()
            last.then_inc(full.sem, full.did(("sS",)))
            emptied(pe, ("sS",))
            tr(room(pe, ("sST",))[:, 0:P], SsT, ident).then_inc(full.sem, full.did(("sST",)))
            pe.wait_ge(smx.sem, smx.at("p"))
            tr(room(pe, ("sPT",))[:, 0:P], Ps, ident).then_inc(full.sem, full.did(("sPT",)))
            emptied(pe, ("sPT",))
            pe.wait_ge(d_vS, 32)
            ps = room(pe, ("sO",))
            for b in range(NS):
                for q in range(KVH):
                    col = slice(b * HA + q * 4, b * HA + q * 4 + 4)
                    last = mm(ps[0:HD, col], vS[:, b, q * HD:(q + 1) * HD], PsT[:, col], start=True, stop=True)
            last.then_inc(full.sem, full.did(("sO",)))
            emptied(pe, ("sO",))
            for g in range(2):
                ps = room(pe, ("sOt", g))
                for i in range(8):
                    last = tr(ps[0:NS, i * HD:(i + 1) * HD], oS[:, 8 * g + i::HA], ident[0:HD, 0:HD])
                last.then_inc(full.sem, full.did(("sOt", g)))

        def sample_gla_pe(pe):
            mm, tr = nc.tensor.matmul, nc.tensor.transpose
            ps = room(pe, ("kSt",))
            for Q in range(2):
                last = tr(ps[0:NS, Q * P:(Q + 1) * P], fmS[:, 8 + Q, :], ident)
            last.then_inc(full.sem, full.did(("kSt",)))
            emptied(pe, ("vb", 0, 3, ST))
            pe.wait_ge(acc_free.sem, acc_free.at(("fmS",)))
            pe.wait_ge(fmz, 1)
            for g in range(2):
                mm(bank[6 + g][0:NS, :], zS[:, :], cst[:, 0:512], start=True, stop=False)
            for b in range(NS):
                for g in range(2):
                    ps = room(pe, ("vB", b, g))
                    mm(ps[:, :], ident[0:NS, b:b + 1].broadcast_to((NS, P)), vog[0:NS, ST, g * 512:(g + 1) * 512], start=True, stop=True)\
                        .then_inc(full.sem, full.did(("vB", b, g)))
                pe.wait_ge(s0n.sem, s0n.at(b))
                for h in range(HB):
                    last = mm(bank[6 + h // 2][0:NS, (h % 2) * DV:(h % 2 + 1) * DV], qz[:, h, b, :], s0[b % 2][:, h, :],
                              start=False, stop=False)
                if b == NS - 1:
                    for g in range(2):
                        last = mm(bank[6 + g][0:NS, :], zS[:, :], cst[:, 0:512], start=False, stop=True)
                last.then_inc(ogb.sem, ogb.did(b))

        def sample_attention_dve(dve):
            v = nc.vector
            TT, TS, STT = v.tensor_tensor, v.tensor_scalar, v.scalar_tensor_tensor
            done = lambda x, key: x.then_inc(evac["dve"].sem, evac["dve"].did(key))
            ps = filled(dve, ("sS",))
            done(TS(SsT, ps[:, 0:P], HD ** -0.5, None, ALU.mult), ("sS",))
            ps = filled(dve, ("sST",))
            done(STT(Ps, distS, slopeS, ps[:, 0:P], ALU.mult, ALU.add), ("sST",))
            dve.drain()
            v.tensor_reduce(smS[:, 0:1], Ps, axis=AX.X, op=ALU.max)
            dve.drain()
            STT(smS[:, 1:2], smS[:, 0:1], -1.0, nsinkP[:, :], ALU.mult, ALU.min)
            dve.drain()
            TT(smS[:, 2:3], smS[:, 1:2], nsinkP[:, :], ALU.subtract).then_inc(smx.sem, smx.did("nm"))
            dve.wait_ge(smp.sem, smp.at("p"))
            TT(smS[:, 5:6], smS[:, 3:4], smS[:, 4:5], ALU.add)
            dve.drain()
            v.reciprocal(smS[:, 5:6], smS[:, 5:6])
            dve.drain()
            TS(Ps, Ps, smS[:, 5:6], None, ALU.mult).then_inc(smx.sem, smx.did("p"))
            ps = filled(dve, ("sPT",))
            done(v.tensor_copy(PsT, ps[:, 0:P]), ("sPT",))
            ps = filled(dve, ("sO",))
            done(v.tensor_copy(oS[:, :], ps[0:HD, 0:P]), ("sO",))
            for g in range(2):
                ps = filled(dve, ("sOt", g))
                done(v.tensor_copy(oa[0:NS, ST, g * 512:(g + 1) * 512], ps[0:NS, :]), ("sOt", g))

        def sample_gla_dve(dve):
            v = nc.vector
            done = lambda x, key: x.then_inc(evac["dve"].sem, evac["dve"].did(key))
            ps = filled(dve, ("kSt",))
            done(v.tensor_copy(kSn[:, :], ps[0:NS, 0:KVH * HD]), ("kSt",))
            dve.drain()
            dve.sem_inc(outs.sem, outs.did("kSn"))
            for b in range(NS):
                dve.wait_ge(s0a.sem, s0a.at(b))
                for g in range(2):
                    key = ("vB", b, g)
                    ps = filled(dve, key)
                    for i in range(2):
                        h = 2 * g + i
                        s = s0[b % 2][:, h, :]
                        last = v.scalar_tensor_tensor(s, ps[:, i * DV:(i + 1) * DV], fmS[:, 14 + h, b:b + 1], s, ALU.mult, ALU.add)
                    done(last, key)
                dve.drain()
                dve.sem_inc(s0n.sem, s0n.did(b))
            dve.wait_ge(ogb.sem, ogb.at(NS - 1))
            for g in range(2):
                last = v.tensor_copy(vog[0:NS, ST, g * 512:(g + 1) * 512], bank[6 + g][0:NS, :])
            dve.drain()
            dve.sem_inc(acc_free.sem, acc_free.did(("ogS",)))

        def route_tile(dve, c, t, R, bufs, gap=lambda: None):
            v = nc.vector
            TT = v.tensor_tensor
            cand, cand2, small = bufs
            cut = lambda lo, n: small[0:R, lo:lo + n]
            some = lambda lo, n: cut(lo, n * PAIRS).rearrange("p (a h k) -> p a h k", a=n, h=PH)
            xf = cut(0, HC * TOPK).rearrange("p (q k) -> p q k", q=HC)
            piu, pif, pij, e01 = some(256, 4).bitcast(u32), some(768, 4), some(1280, 2), some(1536, 2)
            posu = by_head(cut(1792, PAIRS).bitcast(u32))
            vv = val[0:R, t, :, :].rearrange("p (h c) k -> p h c k", c=2)
            sv = by_head(gateS[0:R, :] if R == NS else gate[:, c * TC + t, :])
            cd, cd2, oh = cand[0:R, :, 0:CANDS], cand2[0:R, :, 0:CANDS], onehot[0:R]
            v.tensor_copy(xf, idx[0:R, t, :, :])
            for lo, hi, js, at in ((0, NEAR, TOPK, 0), (NEAR, TOPK, NEAR, NEAR * TOPK)):
                n = hi - lo
                TT(cd[:, :, at:at + n * js].rearrange("p h (i j) -> p h i j", i=n),
                   vv[:, :, 0, lo:hi].rearrange("p h (k o) -> p h k o", o=1).broadcast_to((R, PH, n, js)),
                   vv[:, :, 1:2, 0:js].broadcast_to((R, PH, n, js)), ALU.add)
            dve.drain()
            for h in range(PH):
                v.max(sv[:, h, 0:8], cd[:, h, :])
            dve.drain()
            gap()
            for h in range(PH):
                v.max_index(posu[:, h, 0:8], sv[:, h, 0:8], cd[:, h, :])
            gap()
            for h in range(PH):
                v.match_replace(cd2[:, h, :], sv[:, h, 0:8], cd[:, h, :], -3.0e38)
            dve.drain()
            gap()
            for h in range(PH):
                v.max(sv[:, h, 8:16], cd2[:, h, :])
            dve.drain()
            gap()
            for h in range(PH):
                v.max_index(posu[:, h, 8:16], sv[:, h, 8:16], cd2[:, h, :])
            dve.drain()
            gap()
            v.tensor_single_scalar(piu[:, 0], posu, 4, ALU.logical_shift_right)
            v.tensor_single_scalar(piu[:, 1], posu, 2, ALU.logical_shift_right)
            v.tensor_single_scalar(piu[:, 2], posu, TOPK - NEAR, ALU.bitwise_and)
            v.tensor_single_scalar(piu[:, 3], posu, NEAR - 1, ALU.bitwise_and)
            dve.drain()
            v.tensor_copy(pif, piu)
            dve.drain()
            v.scalar_tensor_tensor(pij[:, 0], pif[:, 1], float(NEAR - TOPK), pif[:, 0], ALU.add, ALU.max)
            v.scalar_tensor_tensor(pij[:, 1], pif[:, 0], float(NEAR), pif[:, 2], ALU.is_lt, ALU.mult)
            dve.drain()
            TT(pij[:, 1], pij[:, 1], pif[:, 3], ALU.add)
            x2 = xf.rearrange("p (h c) k -> p h c k", c=2)
            for half in range(2):
                dve.drain()
                TT(oh, iota[0:R, :].rearrange("p (a b k) -> p a b k", a=1, b=1).broadcast_to((R, PH, TOPK, TOPK)),
                   pij[:, half].rearrange("p h (k o) -> p h k o", o=1).broadcast_to((R, PH, TOPK, TOPK)), ALU.is_equal)
                dve.drain()
                gap()
                TT(oh, oh, x2[:, :, half:half + 1, :].broadcast_to((R, PH, TOPK, TOPK)), ALU.mult)
                dve.drain()
                gap()
                v.tensor_reduce(e01[:, half], oh, axis=AX.X, op=ALU.add)
            dve.drain()
            e = lambda i: e01[:, i].rearrange("p h k -> p (h k)")
            dst = eidS[0:R, :] if R == NS else eidx[:, c * TC + t, :]
            v.scalar_tensor_tensor(dst, e(0), float(NK), e(1), ALU.mult, ALU.add).then_inc(picked.sem, picked.did((c, t)))
            TT(cd[:, :, 0:TOPK], sv, sv[:, :, 0:1].broadcast_to((R, PH, TOPK)), ALU.subtract)
            dve.drain()
            v.tensor_copy(sv, cd[:, :, 0:TOPK])
            dve.drain()

        def gated(c):
            return [(t, P) for t in range(TC)] + ([(ST, NS)] if c == CHUNKS - 1 else [])

        def gates(dve, c, gap=lambda: None):
            v = nc.vector
            dve.sem_inc(sv_ready.sem, sv_ready.did(c))
            dve.wait_ge(ex_ready.sem, ex_ready.at(c))
            for t, R in gated(c):
                sv = by_head(gateS[0:R, :] if R == NS else gate[:, c * TC + t, :])
                v.tensor_reduce(gs[0:R, :], sv, axis=AX.X, op=ALU.add)
                dve.drain()
                v.reciprocal(gs[0:R, :], gs[0:R, :])
                dve.drain()
                v.tensor_tensor(sv, sv, gs[0:R, :].rearrange("p (h o) -> p h o", o=1).broadcast_to((R, PH, TOPK)), ALU.mult)
                dve.drain()
                gap()
            dve.sem_inc(routed.sem, routed.did(c))

        block = ctx.enter_context(nc.Block())

        @block.sync
        def _(sp):
            sp.dma_start(xh[:, 0:TC, :], a["xp"][0:CT, :].rearrange("(t p) d -> p t d", p=P)).then_inc(d_x[0], 16)
            sp.dma_start(xh[0:NS, ST, :], a["xs"]).then_inc(d_x[0], 16)
            sp.dma_start(cst[:, :], a["cst"]).then_inc(d_cst, 16)
            sp.dma_start(g1c[:, :], a["g1c"]).then_inc(d_cst, 16)
            sp.dma_start(wz[:, :, :], a["wz"]).then_inc(d_cst, 16)
            for c in CC:
                for i, (kind, u) in enumerate(UNITS):
                    n = c * NU + i
                    if n >= WR:
                        last = unit_end(c, i - WR) if i >= WR else unit_end(c - 1, NU + i - WR)
                        sp.wait_ge(full.sem, full.at(last))
                    sp.dma_start(wring[:, n % WR, :, :].rearrange("p k c -> p (k c)"), a["w"][i]).then_inc(d_w[n % WR], 16)
                    if n == 0:
                        sp.dma_start(wg[:, :], a["wg"]).then_inc(d_par, 16)
                        sp.dma_start(bg[:, :], a["bg"]).then_inc(d_par, 16)
                        sp.dma_start(nsink[:, :], a["sinks"].partition_broadcast(P)).then_inc(d_par, 16)
                        sp.dma_start(nsinkP[:, :], a["sinksP"]).then_inc(d_par, 16)
                        sp.dma_start(glag[:, :], a["glag"].partition_broadcast(P)).then_inc(d_par, 16)
                        sp.dma_start(kTs[:, :, :, 0:W - 1], a["kTs"]).then_inc(d_kv, 16)
                if c + 1 < CHUNKS:
                    sp.wait_ge(d_scr[c], 64)
                    sp.dma_start(xh[:, 0:TC, :], a["xp"][(c + 1) * CT:(c + 2) * CT, :].rearrange("(t p) d -> p t d", p=P)).then_inc(d_x[c + 1], 16)
            experts_sp(sp)

        @block.gpsimd
        def _(pool):
            g = nc.gpsimd
            g.memset(st1[:, :], 1.0)
            g.memset(stO[:, :, :], 1.0)
            g.memset(kaT[:, :, 0:P], 0.0)
            g.memset(va[:, 0, :], 0.0)
            g.memset(state[:, :, :], 0.0)
            g.memset(qz[:, :, :, :], 0.0)
            g.memset(epst[:, :], EPS)
            g.memset(zS[:, :], 0.0)
            pool.drain()
            pool.sem_inc(init, 1)

            def ga_gate(c, u, p):
                p0, n, R = p
                key = ("ga", c, u, p0)
                pool.wait_ge(sig_ready.sem, sig_ready.at(key))
                x = oa[0:R, p0:p0 + n, u * UC:(u + 1) * UC]
                g.tensor_tensor(x, x, sig[0:R, gate_used[key] % 2, 0:n, :], ALU.mult).then_inc(sig_used.sem, sig_used.did(key))

            issued = [0]

            def early(to):
                while issued[0] < to:
                    e = issued[0]
                    t, k = e // PAIRS, e % PAIRS
                    if e == 0:
                        pool.wait_ge(d_scr[0], 64)
                        pool.wait_ge(d_st[0], 16 * (NS // 2))
                        pool.wait_ge(full.sem, full.at(("n2T", 0, ST, 1)))
                    if k == 0:
                        pool.wait_ge(picked.sem, picked.at((0, t)))
                    if e >= ES:
                        pool.wait_ge(early_used[e % ES], e // ES)
                    pool.indirect_dma_start(out=eslots[e % ES].rearrange("p a d -> p (a d)"), out_offset=None, in_=a["u"],
                                            in_offset=bass.IndirectOffsetOnAxis(ap=eidx[:, t, k:k + 1], axis=0))\
                        .then_inc(early_in[e % ES], 16)
                    if k == ES - 1:
                        pool.dma_start(n2e, o["n2"][t * P:(t + 1) * P, :].rearrange("p (a d) -> p a d", a=2)).then_inc(d_n2e, 16)
                    issued[0] += 1

            def early_before(*point):
                early(min(early_at[point] + ES, TC * PAIRS))

            for c in CC:
                if c == 0:
                    pool.wait_ge(evac["act"].sem, evac["act"].at(("va", 0, 0, ST)))
                    pool.wait_ge(p_ready.sem, p_ready.at((0, NQ - 1)))
                    pool.wait_ge(full.sem, full.at(("PT", 0, NQ - 1, 1)))
                    pool.dma_start(vS[0:W - 1, :, :], a["vc"][:, 1:W, :].rearrange("b s c -> s b c")).then_inc(d_vS, 16)
                    pool.dma_start(vS[W - 1:W, :, :].rearrange("p b c -> p (b c)"), vaS[:, :]).then_inc(d_vS, 16)
                    pool.dma_start(o["ks"][:, 0:W - 1, :], a["kc"][:, 1:W, :]).then_inc(d_out, 16)
                    pool.dma_start(o["vs"][:, 0:W - 1, :], a["vc"][:, 1:W, :]).then_inc(d_out, 16)
                    pool.dma_start(o["vs"][:, W - 1, :], vaS[:, :]).then_inc(d_out, 16)
                for n in range(NG):
                    h, hf = n // 2, n % 2
                    if c:
                        early_before("gla", n, 0)
                    pool.wait_ge(e_ready.sem, e_ready.at((c, n)))
                    if n >= 1:
                        pool.wait_ge(full.sem, full.at(("kdT", c, n - 1)))
                    kb = kbT[:, h:h + 1, hf * 256:(hf + 1) * 256].broadcast_to((P, 8, 256))
                    g.tensor_tensor(Kd, E, kb, ALU.mult).then_inc(k_ready.sem, k_ready.did((c, n)))
                    if c:
                        early_before("gla", n, 3)
                    if n:
                        for p in pair_jobs(c):
                            if (p[0] != 0) == (n - 1) % 2:
                                ga_gate(c, (n - 1) // 2, p)
                if c:
                    early_before("rb", 0)
                for p in pair_jobs(c):
                    if (p[0] != 0) == (NG - 1) % 2:
                        ga_gate(c, (NG - 1) // 2, p)
                pool.dma_start(keysT, a["keysT"]).then_inc(d_keys[c], 16)
                if c == 0:
                    for b in range(NS):
                        if b == 0:
                            pool.wait_ge(sc_ready.sem, sc_ready.at((0, NG - 1, 1)))
                        if b >= 2:
                            pool.wait_ge(ogb.sem, ogb.at(b - 2))
                            pool.wait_ge(s0n.sem, s0n.at(b - 2))
                            pool.dma_start(o["ss"][b - 2].rearrange("h p d -> p h d"), s0[b % 2]).then_inc(d_st[b % 2], 16)
                            pool.wait_ge(d_st[b % 2], 16 * (b // 2))
                        pool.dma_start(s0[b % 2], a["s0"][b].rearrange("h p d -> p h d")).then_inc(d_s0[b % 2], 16)
                    for b in (NS - 2, NS - 1):
                        pool.wait_ge(s0n.sem, s0n.at(b))
                        pool.dma_start(o["ss"][b].rearrange("h p d -> p h d"), s0[b % 2]).then_inc(d_st[b % 2], 16)
                    pool.wait_ge(outs.sem, outs.at("kSn"))
                    pool.dma_start(o["ks"][:, W - 1, :], kSn[:, :]).then_inc(d_out, 16)
                else:
                    pool.wait_ge(outs.sem, outs.at("kwin"))
                    pool.dma_start(o["kp"], kwin).then_inc(d_out, 16)
                    pool.dma_start(o["vp"], va[:, TC, :]).then_inc(d_out, 16)
                    pool.wait_ge(outs.sem, outs.at("state"))
                    pool.dma_start(o["sp"].rearrange("h p d -> p h d"), state[:, :, :]).then_inc(d_out, 16)
                for u in range(4):
                    for p0, n, R in pair_jobs(c):
                        key = ("rb", c, u, p0)
                        x = vog[0:R, p0:p0 + n, u * UC:(u + 1) * UC]
                        if c:
                            early_before("rb", 2 * u + p0 // 2)
                        pool.wait_ge(rb_mul.sem, rb_mul.at(key))
                        g.tensor_tensor(x, x, sig[0:R, gate_used[key] % 2, 0:n, :], ALU.mult).then_inc(sig_used.sem, sig_used.did(key))
                        pool.wait_ge(sig_used.sem, sig_used.at(key))
                        gl = glag[0:R, :].rearrange("p (i d) -> p i d", i=1).broadcast_to((R, n, DV))
                        g.tensor_tensor(x, x, gl, ALU.mult).then_inc(gl_mul.sem, gl_mul.did(key))
                for u in range(4):
                    for p0, n, R in pair_jobs(c):
                        key = ("gb", c, u, p0)
                        x = vog[0:R, p0:p0 + n, u * UC:(u + 1) * UC]
                        if c:
                            early_before("gb", 2 * u + p0 // 2)
                        pool.wait_ge(sig_ready.sem, sig_ready.at(key))
                        pool.wait_ge(gl_mul.sem, gl_mul.at(("rb", c, u, p0)))
                        g.tensor_tensor(x, x, sig[0:R, gate_used[key] % 2, 0:n, :], ALU.mult).then_inc(sig_used.sem, sig_used.did(key))
                pool.wait_ge(sig_used.sem, sig_used.at(key))
                pool.dma_start(g2b, a["g2"].partition_broadcast(P)).then_inc(d_g2[c], 16)
                if c:
                    early_before("n2", 0)
                pool.wait_ge(h_ready.sem, h_ready.at(c))
                pool.dma_start(o["h"][c * CT:(c + 1) * CT, :].rearrange("(t p) d -> p t d", p=P), xh[:, 0:TC, :]).then_inc(d_scr[c], 16)
                if c:
                    early_before("best", 0)
                pool.wait_ge(n2_all.sem, n2_all.at(c))
                pool.dma_start(o["n2"][c * CT:(c + 1) * CT, :].rearrange("(t p) d -> p t d", p=P), oa[:, 0:TC, :]).then_inc(d_scr[c], 16)
                if c == 0:
                    pool.dma_start(o["h"][SEQ:SEQ + NS, :], xh[0:NS, ST, :]).then_inc(d_scr[c], 16)
                    pool.dma_start(o["n2"][SEQ:SEQ + NS, :], oa[0:NS, ST, :]).then_inc(d_scr[c], 16)
            early(TC * PAIRS)
            experts_pool(pool)

        @block.tensor
        def _(pe):
            mm, tr = nc.tensor.matmul, nc.tensor.transpose

            def weights(c, kind, u):
                n = c * NU + UNITS.index((kind, u))
                pe.wait_ge(d_w[n % WR], 16 * (n // WR + 1))
                return wring[:, n % WR, :, :]

            def token_major(c, kind, u, p, lhs, lhs_s):
                p0, n, R = p
                w = wring[:, (c * NU + UNITS.index((kind, u))) % WR, :, :]
                key = (kind, c, u, p0)
                ps = room(pe, key)
                for i in range(n):
                    for k in range(KC):
                        x = lhs_s[:, k, :] if R == NS else lhs[:, k, (p0 + i) * P:(p0 + i + 1) * P]
                        last = mm(ps[0:R, i * UC:(i + 1) * UC], x, w[:, k, :], start=(k == 0), stop=(k == KC - 1))
                last.then_inc(full.sem, full.did(key))
                return last

            def unit(c, kind, u):
                weights(c, kind, u)
                for p in pair_jobs(c):
                    token_major(c, kind, u, p, nT, nTs)

            def turn(key, src, t, R, g):
                ps = room(pe, key)
                for i in range(4):
                    k = 4 * g + i
                    last = tr(ps[:, i * R:(i + 1) * R], src[0:R, t, k * P:(k + 1) * P], ident[0:R, 0:R])
                last.then_inc(full.sem, full.did(key))

            pe.wait_ge(d_cst, 48)
            for c in CC:
                for t, R in tiles_of(c):
                    pe.wait_ge(n_tok.sem, n_tok.at((c, t)))
                    for g in range(2):
                        turn(("nT", c, t, g), oa, t, R, g)
                for t, R in tiles_of(c):
                    emptied(pe, ("nT", c, t, 1))
                for b in range(FMB):
                    if b < 18 and b % 2 == 0:
                        w = weights(c, "fm", b // 2)
                    ps = room(pe, ("fm", c, b))
                    M = P if b < 18 else RANK
                    lhs = [w[:, k, (b % 2) * P:(b % 2 + 1) * P] if b < 18 else wz[:, k, :] for k in range(KC)]
                    if c == 0:
                        for k in range(KC):
                            last = mm(bank[6][0:M, b * NS:(b + 1) * NS], lhs[k], nTs[:, k, :], start=(k == 0), stop=(k == KC - 1))
                        if b == FMB - 1:
                            last.then_inc(acc_full.sem, acc_full.did(("fmS",)))
                    for k in range(KC):
                        last = mm(ps[0:M, :], lhs[k], nT[:, k, :], start=(k == 0), stop=(k == KC - 1))
                    last.then_inc(full.sem, full.did(("fm", c, b)))
                unit(c, "va", 0)
                emptied(pe, ("fm", c, 9))
                for n in range(NQ + 2):
                    if n < NQ:
                        if n % 4 == 0:
                            unit(c, "vb", n // 4)
                        t, q = n // 4, n % 4
                        Q, half = q // 2, q % 2
                        lo = half * 64
                        for g in range(2):
                            ps = room(pe, ("S", c, n, g))
                            for i in range(2):
                                last = mm(ps[:, i * 256:(i + 1) * 256], qaT[lo:lo + 64, 4 * Q + 2 * g + i, t * P:(t + 1) * P],
                                          kaT[lo:lo + 64, Q, t * P:(t + 2) * P], start=True, stop=True)
                            last.then_inc(full.sem, full.did(("S", c, n, g)))
                    if 1 <= n <= NQ:
                        m = n - 1
                        pe.wait_ge(p_ready.sem, p_ready.at((c, m)))
                        for g in range(2):
                            ps = room(pe, ("PT", c, m, g))
                            for i in range(2):
                                for kb in range(2):
                                    j = 2 * i + kb
                                    last = tr(ps[:, j * P:(j + 1) * P], Pb[:, m % 2, 2 * g + i, kb * P:(kb + 1) * P], ident)
                            last.then_inc(full.sem, full.did(("PT", c, m, g)))
                    if n >= 2:
                        m = n - 2
                        t, q = m // 4, m % 4
                        if m == 0:
                            emptied(pe, ("va", c, 0, 2))
                        emptied(pe, ("PT", c, m, 1))
                        ps = room(pe, ("O", c, m))
                        for i in range(4):
                            for kb in range(2):
                                j = (2 * (i % 2) + kb) * P
                                last = mm(ps[:, i * HD:(i + 1) * HD], PT[:, m % 2, i // 2, j:j + P], va[:, t + kb, q * HD:(q + 1) * HD],
                                          start=(kb == 0), stop=(kb == 1))
                        last.then_inc(full.sem, full.did(("O", c, m)))
                if c == 0:
                    sample_attention_pe(pe)
                if c == CHUNKS - 1:
                    ps = room(pe, ("kwin",))
                    for Q in range(2):
                        last = tr(ps[:, Q * P:(Q + 1) * P], kaT[:, Q, CT:CT + P], ident)
                    last.then_inc(full.sem, full.did(("kwin",)))
                pe.wait_ge(d_par, 80)
                emptied(pe, ("fm", c, 18))
                for h in range(HB):
                    ps = room(pe, ("gate", c, h))
                    mm(ps[:, :], wg[:, h * DK:(h + 1) * DK], zbT[:, :], start=True, stop=True)\
                        .then_inc(full.sem, full.did(("gate", c, h)))
                if c == 0:
                    ps = room(pe, ("gateS",))
                    for h in range(HB):
                        last = mm(ps[:, h * NS:(h + 1) * NS], wg[:, h * DK:(h + 1) * DK], fmS[0:RANK, 18, :], start=True, stop=True)
                    last.then_inc(full.sem, full.did(("gateS",)))
                emptied(pe, ("vb", c, 3, 2))
                for n in range(NG):
                    h, hf = n // 2, n % 2
                    pe.wait_ge(q_ready.sem, q_ready.at((c, n)))
                    pe.wait_ge(k_ready.sem, k_ready.at((c, n)))
                    for j in range(2):
                        col = slice(j * P, (j + 1) * P)
                        tok = slice((2 * hf + j) * P, (2 * hf + j + 1) * P)
                        for g in range(2):
                            ps = room(pe, ("L", c, n, j, g))
                            for i in range(4):
                                l = 4 * g + i
                                kk, qq = (Kd[:, l, col], Qd[:, 1 + l, col]) if l < LV else (kbT[:, h, tok], qbT[:, h, tok])
                                last = mm(ps[:, i * P:(i + 1) * P], kk, qq, start=True, stop=True)
                            last.then_inc(full.sem, full.did(("L", c, n, j, g)))
                    ps = room(pe, ("kdT", c, n))
                    for j in range(2):
                        last = tr(ps[:, j * P:(j + 1) * P], Kd[:, 7, j * P:(j + 1) * P], ident)
                    last.then_inc(full.sem, full.did(("kdT", c, n)))
                    emptied(pe, ("kdT", c, n))
                    for j in range(2):
                        t = 2 * hf + j
                        v = vog[:, t, h * DV:(h + 1) * DV]
                        ps = room(pe, ("og", c, n, j))
                        mm(ps[:, 0:DV], scTm(pe, c, n, j), v, start=True, stop=False)
                        if (n, j) != (0, 0):
                            before = (c, n, j - 1) if j else (c, n - 1, 1)
                            emptied(pe, ("st", *before))
                        mm(ps[:, 0:DV], Qd[:, 0, j * P:(j + 1) * P], state[:, h, :], start=False, stop=True)\
                            .then_inc(full.sem, full.did(("og", c, n, j)))
                        ps = room(pe, ("st", c, n, j))
                        mm(ps[:, 0:DV], kdTok[:, j, :], v, start=True, stop=True)\
                            .then_inc(full.sem, full.did(("st", c, n, j)))
                    if n % 2 == 0:
                        weights(c, "ga", n // 2)
                    for p in pair_jobs(c):
                        if (p[0] != 0) == n % 2:
                            token_major(c, "ga", n // 2, p, nT, nTs)
                if c == 0:
                    sample_gla_pe(pe)
                for kind in ("rb", "gb"):
                    for u in range(4):
                        unit(c, kind, u)
                for i, (t, R) in enumerate(tiles_of(c)):
                    if i == 0:
                        pe.wait_ge(u_ready.sem, u_ready.at(c))
                    for g in range(2):
                        turn(("uT", c, t, g), oa, t, R, g)
                for t, R in tiles_of(c):
                    emptied(pe, ("uT", c, t, 1))
                for u in range(4):
                    unit(c, "wo", u)
                for t, R in tiles_of(c):
                    pe.wait_ge(n2_ready.sem, n2_ready.at((c, t)))
                    for g in range(2):
                        turn(("n2T", c, t, g), oa, t, R, g)
                for t, R in tiles_of(c):
                    emptied(pe, ("n2T", c, t, 1))
                pe.wait_ge(d_keys[c], 16)
                for q in range(HC + 1):
                    if q < HC:
                        if q % 2 == 0:
                            w = weights(c, "wq", q // 2)
                        lhs = [w[:, k, (q % 2) * P:(q % 2 + 1) * P] for k in range(KC)]
                        ps = room(pe, ("q", c, q))
                        if c == 0:
                            if q == 0:
                                pe.wait_ge(acc_free.sem, acc_free.at(("ogS",)))
                            for k in range(KC):
                                last = mm(bank[6][:, q * NS:(q + 1) * NS], lhs[k], nTs[:, k, :], start=(k == 0), stop=(k == KC - 1))
                            if q == HC - 1:
                                last.then_inc(acc_full.sem, acc_full.did(("qS",)))
                        for k in range(KC):
                            last = mm(ps[:, :], lhs[k], nT[:, k, :], start=(k == 0), stop=(k == KC - 1))
                        last.then_inc(full.sem, full.did(("q", c, q)))
                    if q >= 1:
                        m = q - 1
                        emptied(pe, ("q", c, m))
                        ps = room(pe, ("s", c, m))
                        for t in range(TC):
                            last = mm(ps[:, t * P:(t + 1) * P], qh[:, m % 2, t * P:(t + 1) * P], keysT[:, m, :], start=True, stop=True)
                        last.then_inc(full.sem, full.did(("s", c, m)))
                if c == 0:
                    pe.wait_ge(qS_ready, 1)
                    for g in range(4):
                        ps = room(pe, ("sR", g))
                        for i in range(4):
                            last = mm(ps[0:NS, i * P:(i + 1) * P], qSs[:, 4 * g + i, :], keysT[:, 4 * g + i, :], start=True, stop=True)
                        last.then_inc(full.sem, full.did(("sR", g)))
            experts_pe(pe)

        @block.scalar
        def _(act):
            A = nc.scalar.activation

            def copy(dst, key, src, scale=1.0):
                A(dst, src, ACT.Copy, scale=scale).then_inc(evac["act"].sem, evac["act"].did(key))

            def norm_stats(c, i, src, junk):
                for t, R in tiles_of(c):
                    A(junk[0:R, t, :], src[0:R, t, :], ACT.Square, accum_out=st1[0:R, t:t + 1])
                act.drain()
                A(rs1[:, :], st1[:, :], ACT.Sqrt, scale=1.0 / D, bias=epst[:, 0:1]).then_inc(ss1.sem, ss1.did((c, i)))

            def evac_turn(kind, c, g, t, R):
                key = (kind, c, t, g)
                ps = filled(act, key)
                dst = nT[:, 4 * g:4 * g + 4, t * P:(t + 1) * P] if R == P else nTs[:, 4 * g:4 * g + 4, :]
                copy(dst, key, ps[:, 0:4 * R].rearrange("p (k r) -> p k r", k=4))

            def sigmoid(kind, c, u, p):
                p0, n, R = p
                key = (kind, c, u, p0)
                ps = filled(act, key)
                s = gate_used[key]
                if s >= 2:
                    before = gates_k[s - 2]
                    act.wait_ge(sig_used.sem, sig_used.at(before))
                x = A(sig[0:R, s % 2, 0:n, :], ps[0:R, 0:n * UC].rearrange("p (i c) -> p i c", i=n), ACT.Sigmoid)
                x.then_inc(sig_ready.sem, sig_ready.did(key))
                if kind != "rb":
                    act.wait_ge(sig_ready.sem, sig_ready.at(key))
                    act.sem_inc(evac["act"].sem, evac["act"].did(key))

            def route_exp(c):
                act.wait_ge(sv_ready.sem, sv_ready.at(c))
                A(gate[:, c * TC:(c + 1) * TC, :], gate[:, c * TC:(c + 1) * TC, :], ACT.Exp)
                if c == CHUNKS - 1:
                    A(gateS[:, :], gateS[:, :], ACT.Exp)
                act.drain()
                act.sem_inc(ex_ready.sem, ex_ready.did(c))

            act.wait_ge(init, 1)
            for c in CC:
                act.wait_ge(d_x[c], 32 if c == 0 else 16)
                if c:
                    act.wait_ge(d_scr[c - 1], 64)
                norm_stats(c, 0, xh, oa)
                for b in range(FMB):
                    ps = filled(act, ("fm", c, b))
                    if b < 8:
                        if b == 0 and c:
                            act.wait_ge(evac["dve"].sem, evac["dve"].at(("s", c - 1, HC - 1)))
                            if c == 1:
                                act.wait_ge(evac["dve"].sem, evac["dve"].at(("sR", 3)))
                        copy(qaT[:, b, :], ("fm", c, b), ps[:, :], HD ** -0.5)
                    elif b < 10:
                        if b == 8 and c:
                            A(kaT[:, :, 0:P], kaT[:, :, CT:CT + P], ACT.Copy)
                            act.drain()
                        copy(kaT[:, b - 8, P:P + CT], ("fm", c, b), ps[:, :])
                    elif b < 14:
                        copy(qbT[:, b - 10, :], ("fm", c, b), ps[:, :], DK ** -0.5)
                    elif b < 18:
                        copy(kbT[:, b - 14, :], ("fm", c, b), ps[:, :])
                    else:
                        copy(zbT[:, :], ("fm", c, b), ps[0:RANK, :])
                if c:
                    A(va[:, 0, :], va[:, TC, :], ACT.Copy)
                    act.drain()
                for p0, n, R in pair_jobs(c):
                    key = ("va", c, 0, p0)
                    ps = filled(act, key)
                    if R == P:
                        copy(va[:, 1 + p0:1 + p0 + n, :], key, ps[:, 0:n * UC].rearrange("p (i c) -> p i c", i=n))
                    else:
                        copy(vaS[:, :], key, ps[0:R, 0:UC])

                def vb(u):
                    for p0, n, R in pair_jobs(c):
                        key = ("vb", c, u, p0)
                        ps = filled(act, key)
                        copy(vog[0:R, p0:p0 + n, u * UC:(u + 1) * UC], key, ps[0:R, 0:n * UC].rearrange("p (i c) -> p i c", i=n))

                if c:
                    route_exp(c - 1)
                    act.wait_ge(routed.sem, routed.at(c - 1))
                for n in range(NQ + 1):
                    if n < NQ:
                        if n % 4 == 0:
                            vb(n // 4)
                    if n >= 1:
                        for g in range(2):
                            key = ("PT", c, n - 1, g)
                            if n >= 3:
                                act.wait_ge(full.sem, full.at(("O", c, n - 3)))
                            ps = filled(act, key)
                            copy(PT[:, (n - 1) % 2, g, :], key, ps[:, :])
                    if n < NQ:
                        act.wait_ge(nm_ready.sem, nm_ready.at((c, n)))
                        s = n % 4
                        for i in range(4):
                            A(Pb[:, n % 2, i, :], Pb[:, n % 2, i, :], ACT.Exp, bias=nm[:, s, i:i + 1], accum_out=rsum[:, s, i:i + 1])
                        A(esink[:, s, :], sk[:, s, :], ACT.Exp)
                        act.drain()
                        act.sem_inc(p_ready.sem, p_ready.did((c, n)))
                if c == 0:
                    act.wait_ge(smx.sem, smx.at("nm"))
                    A(Ps, Ps, ACT.Exp, bias=smS[:, 1:2], accum_out=smS[:, 3:4])
                    A(smS[:, 4:5], smS[:, 2:3], ACT.Exp)
                    act.drain()
                    act.sem_inc(smp.sem, smp.did("p"))
                act.wait_ge(y_ready.sem, y_ready.at(c))
                A(Tt, Y, ACT.Abs)
                if c == 0:
                    act.wait_ge(aS_in, 1)
                    A(tS[:, :, :], yS[:, :, :], ACT.Abs)
                act.drain()
                A(Tt, Tt, ACT.Exp, scale=-1.0)
                if c == 0:
                    A(tS[:, :, :], tS[:, :, :], ACT.Exp, scale=-1.0)
                act.drain()
                A(Tt, Tt, ACT.Ln, bias=1.0).then_inc(t_ready.sem, t_ready.did(c))
                if c == 0:
                    A(tS[:, :, :], tS[:, :, :], ACT.Ln, bias=1.0).then_inc(aS_out, 1)
                    act.wait_ge(aS_in, 2)
                    A(aS[:, :, :], yS[:, :, :], ACT.Exp, scale=1.0 / GATE_TEMP)
                def decays(n):
                    h, hf = n // 2, n % 2
                    act.wait_ge(d_ready.sem, d_ready.at((c, n)))
                    if n == 0:
                        act.drain()
                    A(E0[n % 2], bT[:, h, hf * 256:(hf + 1) * 256], ACT.Exp, scale=1.0 / GATE_TEMP)
                    A(E, E, ACT.Exp, scale=1.0 / GATE_TEMP)
                    act.drain()
                    act.sem_inc(e_ready.sem, e_ready.did((c, n)))

                decays(0)
                for n in range(NG):
                    h, hf = n // 2, n % 2
                    key = ("kdT", c, n)
                    ps = filled(act, key)
                    if n:
                        act.wait_ge(full.sem, full.at(("st", c, n - 1, 1)))
                    copy(kdTok[:, :, :], key, ps[:, 0:2 * P].rearrange("p (j c) -> p j c", j=2))
                    for j in range(2):
                        key = ("og", c, n, j)
                        ps = filled(act, key)
                        act.wait_ge(full.sem, full.at(("st", c, n, j)))
                        copy(vog[:, 2 * hf + j, h * DV:(h + 1) * DV], key, ps[:, 0:DV])
                    if n + 1 < NG:
                        decays(n + 1)
                    for p in pair_jobs(c):
                        if (p[0] != 0) == n % 2:
                            sigmoid("ga", c, n // 2, p)
                if c == 0:
                    act.drain()
                    for b in range(NS):
                        act.wait_ge(d_s0[b % 2], 16 * (b // 2 + 1))
                        for h in range(HB):
                            last = A(s0[b % 2][:, h, :], s0[b % 2][:, h, :], ACT.Copy, scale=aS[:, h, b:b + 1])
                        act.drain()
                        act.sem_inc(s0a.sem, s0a.did(b))
                    act.wait_ge(acc_free.sem, acc_free.at(("ogS",)))
                emptied(act, ("st", c, NG - 1, 1))
                act.drain()
                for t, R in tiles_of(c):
                    for h in range(HB):
                        A(junkO[0:R, t, h, :], vog[0:R, t, h * DV:(h + 1) * DV], ACT.Square, accum_out=stO[0:R, t, h:h + 1])
                act.drain()
                A(rsO[:, :, :], stO[:, :, :], ACT.Sqrt, scale=1.0 / DV, bias=epst[:, 0:1]).then_inc(ssO.sem, ssO.did(c))
                for kind in ("rb", "gb"):
                    for u in range(4):
                        for p in pair_jobs(c):
                            sigmoid(kind, c, u, p)
                for t, R in tiles_of(c):
                    for g in range(2):
                        evac_turn("uT", c, g, t, R)
                act.wait_ge(h_ready.sem, h_ready.at(c))
                norm_stats(c, 1, xh, vog)
                for t, R in tiles_of(c):
                    for g in range(2):
                        evac_turn("n2T", c, g, t, R)
                for q in range(HC):
                    ps = filled(act, ("q", c, q))
                    if q >= 2:
                        act.wait_ge(full.sem, full.at(("s", c, q - 2)))
                    copy(qh[:, q % 2, :], ("q", c, q), ps[:, :])
            experts_act(act, route_exp)

        @block.vector
        def _(dve):
            v = nc.vector
            TT, TS, STT = v.tensor_tensor, v.tensor_scalar, v.scalar_tensor_tensor

            def done(x, key):
                return x.then_inc(evac["dve"].sem, evac["dve"].did(key))

            def rows(ap, R):
                return ap[0:R]

            multiplied, points = [0], []

            def early(*point):
                k = len(points)
                points.append(point)
                assert EARLY[k][0] == point or EARLY[k][0] == point + (k,)
                products(EARLY[k][1])

            def products(rows):
                for e in range(multiplied[0], multiplied[0] + rows):
                    if e % PAIRS == 0:
                        dve.wait_ge(d_n2e, 16 * (e // PAIRS + 1))
                    dve.wait_ge(early_in[e % ES], 16 * (e // ES + 1))
                    v.tensor_tensor_reduce(out=eslots[e % ES], in0=eslots[e % ES], in1=n2e, scale=1.0, scalar=0.0, op0=ALU.mult,
                                           op1=ALU.add, accum_out=early_dots[:, e:e + 1]).then_inc(early_used[e % ES], 1)
                multiplied[0] += rows

            dve.wait_ge(init, 1)
            dve.wait_ge(d_cst, 48)
            dve.wait_ge(d_par, 80)
            TS(nsink[:, :], nsink[:, :], -1.0, None, ALU.mult)
            TS(nsinkP[:, :], nsinkP[:, :], -1.0, None, ALU.mult)
            for c in CC:
                dve.wait_ge(ss1.sem, ss1.at((c, 0)))
                v.reciprocal(rs1[:, :], rs1[:, :])
                dve.drain()
                for t, R in tiles_of(c):
                    TS(oa[0:R, t, :], xh[0:R, t, :], rs1[0:R, t:t + 1], None, ALU.mult).then_inc(n_tok.sem, n_tok.did((c, t)))
                for t, R in tiles_of(c):
                    for g in range(2):
                        key = ("nT", c, t, g)
                        ps = filled(dve, key)
                        dst = nT[:, 4 * g:4 * g + 4, t * P:(t + 1) * P] if R == P else nTs[:, 4 * g:4 * g + 4, :]
                        gain = g1c[:, 4 * g:4 * g + 4].rearrange("p (k o) -> p k o", o=1).broadcast_to((P, 4, R))
                        if g == 0 and t == 0 and c:
                            pass
                        done(TT(dst, ps[:, 0:4 * R].rearrange("p (k r) -> p k r", k=4), gain, ALU.mult), key)
                if c:
                    dve.wait_ge(d_out, 64)
                    for t in range(TC):
                        route_tile(dve, c - 1, t, P, route_bufs[0], (lambda: early("route")) if t else (lambda: None))
                    gates(dve, c - 1, lambda: early("route"))
                if c == 0:
                    dve.wait_ge(acc_full.sem, acc_full.at(("fmS",)))
                    v.tensor_copy(fmS[:, 0:18, :], bank[6][:, 0:18 * NS].rearrange("p (b s) -> p b s", b=18))
                    v.tensor_copy(fmS[0:RANK, 18, :], bank[6][0:RANK, 18 * NS:19 * NS]).then_inc(acc_free.sem, acc_free.did(("fmS",)))
                    dve.drain()
                    dve.wait_ge(d_kv, 16)
                    for Q in range(2):
                        last = v.tensor_copy(kTs[:, Q, :, W - 1], fmS[:, 8 + Q, :])
                    last.then_inc(knew, 1)
                    for b in range(NS):
                        last = TS(qz[:, :, b, b], fmS[:, 10:14, b], DK ** -0.5, None, ALU.mult)
                    last.then_inc(fmz, 1)
                    dve.drain()
                for n in range(NQ + 2):
                    if n < NQ:
                        t, q, s = n // 4, n % 4, n % 4
                        for g in range(2):
                            key = ("S", c, n, g)
                            ps = filled(dve, key)
                            if g == 0 and n >= 2:
                                dve.wait_ge(full.sem, full.at(("PT", c, n - 2, 1)))
                            for i in range(2):
                                last = STT(Pb[:, n % 2, 2 * g + i, :], dist, SL[4 * q + 2 * g + i], ps[:, i * 256:(i + 1) * 256],
                                           ALU.mult, ALU.add)
                            done(last, key)
                            if c:
                                early("scores", n, g)
                        dve.drain()
                        if c == 0 and t == 0:
                            v.memset(Pb[:, n % 2, :, 0:P], NEG)
                            dve.drain()
                        v.tensor_reduce(mx[:, s, :], Pb[:, n % 2, :, :], axis=AX.X, op=ALU.max)
                        dve.drain()
                        if c:
                            early("scores", n, 2)
                        STT(nm[:, s, :], mx[:, s, :], -1.0, nsink[:, 4 * q:4 * q + 4], ALU.mult, ALU.min)
                        dve.drain()
                        TT(sk[:, s, :], nm[:, s, :], nsink[:, 4 * q:4 * q + 4], ALU.subtract).then_inc(nm_ready.sem, nm_ready.did((c, n)))
                        if c:
                            early("scores", n, 3)
                    if n >= 2:
                        m = n - 2
                        t, q, s = m // 4, m % 4, m % 4
                        key = ("O", c, m)
                        ps = filled(dve, key)
                        TT(rden[:, s, :], rsum[:, s, :], esink[:, s, :], ALU.add)
                        dve.drain()
                        if c:
                            early("values", m, 0)
                        v.reciprocal(rden[:, s, :], rden[:, s, :])
                        dve.drain()
                        done(TT(oa[:, t, q * 256:(q + 1) * 256].rearrange("p (i d) -> p i d", i=4),
                                ps[:, 0:256].rearrange("p (i d) -> p i d", i=4),
                                rden[:, s, :].rearrange("p (i o) -> p i o", o=1).broadcast_to((P, 4, HD)), ALU.mult), key)
                        if c:
                            early("values", m, 1)
                if c == 0:
                    sample_attention_dve(dve)
                if c == CHUNKS - 1:
                    ps = filled(dve, ("kwin",))
                    done(v.tensor_copy(kwin, ps[:, 0:KVH * HD]), ("kwin",))
                    dve.wait_ge(evac["dve"].sem, evac["dve"].at(("kwin",)))
                    dve.sem_inc(outs.sem, outs.did("kwin"))
                for h in range(HB):
                    ps = filled(dve, ("gate", c, h))
                    done(TS(Y[:, h, :], ps[:, :], bg[:, h:h + 1], None, ALU.add), ("gate", c, h))
                dve.drain()
                dve.sem_inc(y_ready.sem, y_ready.did(c))
                if c == 0:
                    ps = filled(dve, ("gateS",))
                    done(TT(yS[:, :, :], ps[:, 0:HB * NS].rearrange("p (h b) -> p h b", h=HB),
                            bg[:, :].rearrange("p (h o) -> p h o", o=1).broadcast_to((P, HB, NS)), ALU.add), ("gateS",))
                    dve.drain()
                    dve.sem_inc(aS_in, 1)
                dve.wait_ge(t_ready.sem, t_ready.at(c))
                STT(Y, Y, 0.0, Tt, ALU.min, ALU.subtract)
                if c == 0:
                    dve.wait_ge(aS_out, 1)
                    STT(yS[:, :, :], yS[:, :, :], 0.0, tS[:, :, :], ALU.min, ALU.subtract).then_inc(aS_in, 1)
                dve.drain()
                for h in range(HB):
                    for t in range(TC):
                        v.tensor_tensor_scan(bT[:, h, t * P:(t + 1) * P], ones, Y[:, h, t * P:(t + 1) * P], 0.0, ALU.mult, ALU.add)
                dve.drain()

                def differences(n):
                    h, hf = n // 2, n % 2
                    b = bT[:, h, hf * 256:(hf + 1) * 256]
                    for l in range(LV):
                        m = (P // 2) >> l
                        e = E[:, l, :].rearrange("p (n two m) -> p n two m", two=2, m=m)
                        bb = b.rearrange("p (n two m) -> p n two m", two=2, m=m)
                        edge = bb[:, :, 0, m - 1:m].broadcast_to((P, P // m, m))
                        TT(e[:, :, 1, :], bb[:, :, 1, :], edge, ALU.subtract)
                        TT(e[:, :, 0, :], edge, bb[:, :, 0, :], ALU.subtract)
                    b2 = b.rearrange("p (j t) -> p j t", j=2)
                    TT(E[:, 7, :].rearrange("p (j t) -> p j t", j=2), b2[:, :, P - 1:P].broadcast_to((P, 2, P)), b2, ALU.subtract)
                    dve.drain()
                    dve.sem_inc(d_ready.sem, d_ready.did((c, n)))

                for n in range(NG):
                    h, hf = n // 2, n % 2
                    if n == 0:
                        differences(0)
                    dve.wait_ge(e_ready.sem, e_ready.at((c, n)))
                    if n:
                        dve.wait_ge(full.sem, full.at(("og", c, n - 1, 1)))
                    qb = qbT[:, h:h + 1, hf * 256:(hf + 1) * 256]
                    TT(Qd[:, 1:8, :], E[:, 0:7, :], qb.broadcast_to((P, 7, 256)), ALU.mult)
                    TT(Qd[:, 0:1, :], E0[n % 2].rearrange("p (o t) -> p o t", o=1), qb, ALU.mult)
                    dve.drain()
                    dve.sem_inc(q_ready.sem, q_ready.did((c, n)))
                    if c:
                        early("gla", n, 0)
                    for j in range(2):
                        for g in range(2):
                            key = ("L", c, n, j, g)
                            ps = filled(dve, key)
                            done(TT(M1[:, 4 * g:4 * g + 4, :], ps[:, :].rearrange("p (l t) -> p l t", l=4), masks[:, 4 * g:4 * g + 4, :],
                                    ALU.mult), key)
                        dve.drain()
                        if c:
                            early("gla", n, 1 + 2 * j)
                        if n:
                            dve.wait_ge(full.sem, full.at(("og", c, n - 1, j)))
                        v.tensor_reduce(scT[:, j, :], M1.rearrange("p l t -> p t l"), axis=AX.X, op=ALU.add)\
                            .then_inc(sc_ready.sem, sc_ready.did((c, n, j)))
                        dve.drain()
                        if c:
                            early("gla", n, 2 + 2 * j)
                    for j in range(2):
                        key = ("st", c, n, j)
                        ps = filled(dve, key)
                        done(STT(state[:, h, :], state[:, h, :], E0[n % 2][:, j * P + P - 1:j * P + P], ps[:, 0:DV], ALU.mult, ALU.add), key)
                        dve.drain()
                        if c:
                            early("gla", n, 5 + j)
                    if n + 1 < NG:
                        dve.wait_ge(k_ready.sem, k_ready.at((c, n)))
                        differences(n + 1)
                    if c:
                        early("gla", n, 7)
                if c == 0:
                    sample_gla_dve(dve)
                else:
                    dve.sem_inc(outs.sem, outs.did("state"))
                if c:
                    early("norm", 0)
                dve.wait_ge(ssO.sem, ssO.at(c))
                v.reciprocal(rsO[:, :, :], rsO[:, :, :])
                dve.drain()
                for u in range(4):
                    for p0, n, R in pair_jobs(c):
                        key = ("rb", c, u, p0)
                        ps = filled(dve, key)
                        dve.wait_ge(sig_ready.sem, sig_ready.at(key))
                        for i in range(n):
                            x = vog[0:R, p0 + i, u * UC:(u + 1) * UC]
                            last = STT(x, x, rsO[0:R, p0 + i, u:u + 1], ps[0:R, i * UC:(i + 1) * UC], ALU.mult, ALU.mult)
                        done(last, key)
                        dve.drain()
                        dve.sem_inc(rb_mul.sem, rb_mul.did(key))
                        if c:
                            early("rb", 2 * u + p0 // 2)
                for u in range(4):
                    for p0, n, R in pair_jobs(c):
                        key = ("gb", c, u, p0)
                        if c:
                            early("gb", 2 * u + p0 // 2)
                        dve.wait_ge(sig_used.sem, sig_used.at(key))
                        x = vog[0:R, p0:p0 + n, u * UC:(u + 1) * UC]
                        y = oa[0:R, p0:p0 + n, u * UC:(u + 1) * UC]
                        TT(y, y, x, ALU.add)
                dve.drain()
                dve.sem_inc(u_ready.sem, u_ready.did(c))
                if c:
                    early("merged", 0)
                for u in range(4):
                    for p0, n, R in pair_jobs(c):
                        key = ("wo", c, u, p0)
                        ps = filled(dve, key)
                        x = xh[0:R, p0:p0 + n, u * UC:(u + 1) * UC]
                        done(TT(x, ps[0:R, 0:n * UC].rearrange("p (i c) -> p i c", i=n), x, ALU.add), key)
                        if c and u < 3:
                            early("wo", 2 * u + p0 // 2)
                dve.drain()
                dve.sem_inc(h_ready.sem, h_ready.did(c))
                if c:
                    early("n2", 0)
                dve.wait_ge(ss1.sem, ss1.at((c, 1)))
                dve.wait_ge(d_g2[c], 16)
                v.reciprocal(rs1[:, :], rs1[:, :])
                dve.drain()
                for t, R in tiles_of(c):
                    STT(oa[0:R, t, :], xh[0:R, t, :], rs1[0:R, t:t + 1], g2b[0:R, :], ALU.mult, ALU.mult)\
                        .then_inc(n2_ready.sem, n2_ready.did((c, t)))
                dve.drain()
                dve.sem_inc(n2_all.sem, n2_all.did(c))
                if c:
                    early("n2", 1)

                def best(ps, n, R, t0, q, key):
                    src = lambda t: ps[0:R, t * P:(t + 1) * P]
                    at = lambda buf, t, lo: (buf[0:R, t0, q + t, lo:lo + 8] if t0 == ST else buf[0:R, t, q, lo:lo + 8])
                    for t in range(n):
                        v.max(at(val, t, 0), src(t))
                    dve.drain()
                    for t in range(n):
                        v.max_index(at(idx, t, 0), at(val, t, 0), src(t))
                        last = v.match_replace(tmp[0:R, t, :], at(val, t, 0), src(t), -3.0e38)
                    done(last, key)
                    dve.drain()
                    for t in range(n):
                        v.max(at(val, t, 8), tmp[0:R, t, :])
                    dve.drain()
                    for t in range(n):
                        v.max_index(at(idx, t, 8), at(val, t, 8), tmp[0:R, t, :])
                    dve.drain()

                for q in range(HC):
                    key = ("s", c, q)
                    if c == 0 and q == HC - 1:
                        pass
                    best(filled(dve, key), TC, P, 0, q, key)
                    if c:
                        early("best", q)
                if c == 0:
                    dve.wait_ge(acc_full.sem, acc_full.at(("qS",)))
                    v.tensor_copy(qSs[:, :, :], bank[6][:, 0:HC * NS].rearrange("p (q b) -> p q b", q=HC)).then_inc(qS_ready, 1)
                    for g in range(4):
                        key = ("sR", g)
                        best(filled(dve, key), 4, NS, ST, 4 * g, key)
            products(TC * PAIRS - multiplied[0])
            experts_dve(dve)

OUTS = {"yp": (SEQ, D), "ys": (NS, D), "kp": (W, KVH * HD), "vp": (W, KVH * HD), "sp": (HB, DK, DV),
        "ks": (NS, W, KVH * HD), "vs": (NS, W, KVH * HD), "ss": (NS, HB, DK, DV)}


def unit_columns():
    q = np.arange(HA * HD).reshape(2, 2, 4, HD).transpose(0, 2, 1, 3).ravel()
    at = HA * HD
    cols = {"k": np.arange(at, at + KVH * HD)}
    at += KVH * HD
    cols["va"] = np.arange(at, at + KVH * HD)
    at += KVH * HD
    for name, n in (("qb", HB * DK), ("kb", HB * DK), ("vb", HB * DV), ("rb", HB * DV), ("z", RANK), ("ga", D), ("gb", D)):
        cols[name] = np.arange(at, at + n)
        at += n
    cols["fm"] = np.concatenate([q, cols["k"], cols["qb"], cols["kb"]])
    return cols


def kernel(**inputs):
    import concourse.bacc as bacc
    from concourse.bass_utils import run_bass_kernel_spmd

    x = {k: np.asarray(v) for k, v in inputs.items()}
    f = np.ascontiguousarray
    w_in, w_out, wq = x["w_in"][0], x["w_out"][0], x["peer_wq"][0]
    cols = unit_columns()
    units = []
    for kind, u in UNITS:
        w = w_out if kind == "wo" else wq if kind == "wq" else w_in[:, cols[kind]]
        units.append(w[:, u * UC:(u + 1) * UC].reshape(KC, P, UC).transpose(1, 0, 2).reshape(P, KC * UC))
    kc = x["cache_k_win"][0].reshape(NS, W, KVH * HD)
    vc = x["cache_v_win"][0].reshape(NS, W, KVH * HD)
    arrays = {
        "xp": f(x["x_prompt"][0]), "xs": f(x["x_sample"][:, 0]), "cst": constants(), "w": f(np.stack(units)),
        "g1c": f(x["norm1_g"][0].reshape(KC, P).T), "wz": f(w_in[:, cols["z"]].reshape(KC, P, RANK).transpose(1, 0, 2)),
        "wg": f(x["w_gla_gate"][0]), "bg": f(x["b_gla_gate"][0].reshape(HB, DK).T), "sinks": f(x["attn_sinks"][0]),
        "sinksP": f(np.tile(x["attn_sinks"][0], NS)[:, None]), "g2": f(x["norm2_g"][0]), "glag": f(x["gla_norm_g"][0]),
        "gf": f(x["final_norm_g"]), "kc": f(kc), "vc": f(vc),
        "kTs": f(kc[:, 1:].reshape(NS, W - 1, 2, P).transpose(3, 2, 0, 1)),
        "keysT": f(x["peer_subkeys"][0].reshape(HC, NK, P).transpose(2, 0, 1)),
        "s0": f(x["state_gla"][0]), "u": f(x["peer_u"][0]), "v": f(x["peer_v"][0]),
    }
    nc = bacc.Bacc("TRN2", target_bir_lowering=False, num_devices=1)
    dt = mybir.dt.float32
    a = {k: nc.dram_tensor(f"in_{k}", v.shape, dt, kind="ExternalInput").ap() for k, v in arrays.items()}
    o = {k: nc.dram_tensor(f"out_{k}", s, dt, kind="ExternalOutput").ap() for k, s in OUTS.items()}
    for k in ("h", "n2"):
        o[k] = nc.dram_tensor(f"scratch_{k}", (SEQ + NS, D), dt, kind="Internal").ap()
    build(nc, a, o)
    r = run_bass_kernel_spmd(nc, [{f"in_{k}": v for k, v in arrays.items()}], core_ids=[0]).results[0]
    r = {k: r[f"out_{k}"] for k in OUTS}
    kv = (1, -1, W, KVH, HD)
    return (r["yp"].reshape(1, SEQ, D), r["ys"].reshape(NS, 1, D), r["kp"].reshape(kv), r["vp"].reshape(kv),
            r["sp"].reshape(1, 1, HB, DK, DV), r["ks"].reshape(kv), r["vs"].reshape(kv), r["ss"].reshape(1, NS, HB, DK, DV))
```
